# Optimizing a Trainium2 kernel written in Bass

```python
import math
import jax, jax.numpy as jnp
from jax import lax
import numpy as np

D_MODEL = 1024
BATCH = 1
SEQ = 1024
DEPTH = 1

N_MIXERS = 2
N_CONV_LAYERS = (DEPTH + N_MIXERS - 1) // N_MIXERS
N_ATTN_LAYERS = DEPTH // N_MIXERS

CONV_KERNEL = 31
CONV_EXPAND = 2

HEAD_DIM = 128
HEADS_PER_GROUP = D_MODEL // HEAD_DIM
DILATED_GROUPS = ((128, 1), (512, 4), (2048, 16))
N_GROUPS = len(DILATED_GROUPS)
N_TOTAL_HEADS = N_GROUPS * HEADS_PER_GROUP
GROUP_WIDTH = HEADS_PER_GROUP * HEAD_DIM
QKV_WIDTH = N_GROUPS * 3 * GROUP_WIDTH
BLOCK = 128
ALIBI_MAX = 8.0

D_FF = 2816
FFN_KERNEL = 3
EPS = 1e-6

kernel_name = "hybrid_conformer_dilated_attn_convffn"

def rmsnorm(x, g):
    xf = x.astype(jnp.float32)
    y = xf * lax.rsqrt(jnp.mean(xf * xf, axis=-1, keepdims=True) + EPS)
    return (y * g.astype(jnp.float32)).astype(x.dtype)

def layernorm(x, g, b):
    xf = x.astype(jnp.float32)
    mu = jnp.mean(xf, axis=-1, keepdims=True)
    var = jnp.mean(jnp.square(xf - mu), axis=-1, keepdims=True)
    y = (xf - mu) * lax.rsqrt(var + EPS)
    return (y * g.astype(jnp.float32) + b.astype(jnp.float32)).astype(x.dtype)

def causal_dwconv(x, w, b):
    k, c = w.shape
    y = lax.conv_general_dilated(
        x, w.astype(x.dtype)[:, None, :], window_strides=(1,), padding=[(k - 1, 0)],
        dimension_numbers=("NWC", "WIO", "NWC"), feature_group_count=c)
    return y + b.astype(x.dtype)

def conformer_conv_module(h, w_in, b_in, dw, dw_b, ln_g, ln_b, w_out, b_out):
    u = h @ w_in + b_in
    a, g = jnp.split(u, 2, axis=-1)
    u = a * jax.nn.sigmoid(g)
    u = causal_dwconv(u, dw, dw_b)
    u = jax.nn.silu(layernorm(u, ln_g, ln_b))
    return u @ w_out + b_out

def dilated_branch(q, k, v, slopes, window, dilation):
    b, s, h, dh = q.shape
    n_back = window // dilation
    L = s // dilation
    nb = -(-L // BLOCK)
    Lp = nb * BLOCK
    n = b * dilation

    def to_sub(t):
        t = t.reshape(b, L, dilation, h, dh).transpose(0, 2, 1, 3, 4).reshape(n, L, h, dh)
        return jnp.pad(t, ((0, 0), (0, Lp - L), (0, 0), (0, 0)))

    def windows(t):
        t = jnp.pad(t, ((0, 0), (BLOCK, 0), (0, 0), (0, 0))).reshape(n, nb + 1, BLOCK, h, dh)
        return jnp.concatenate([t[:, :-1], t[:, 1:]], axis=2)

    qb = to_sub(q).reshape(n, nb, BLOCK, h, dh).astype(jnp.float32)
    kw = windows(to_sub(k)).astype(jnp.float32)
    vw = windows(to_sub(v)).astype(jnp.float32)

    scores = jnp.einsum("nbqhd,nbkhd->nbhqk", qb, kw) * (dh ** -0.5)
    qi = jnp.arange(BLOCK)[:, None]
    ki = jnp.arange(2 * BLOCK)[None, :]
    delta = qi + BLOCK - ki
    key_idx = jnp.arange(nb)[:, None, None] * BLOCK + ki[None] - BLOCK
    valid = (delta >= 0)[None] & (delta <= n_back)[None] & (key_idx >= 0)
    bias = -slopes.astype(jnp.float32)[:, None, None] * (delta * dilation).astype(jnp.float32)[None]
    scores = jnp.where(valid[None, :, None], scores + bias[None, None], -1e30)

    m = jnp.max(scores, axis=-1, keepdims=True)
    p = jnp.exp(scores - m)
    den = jnp.sum(p, axis=-1)
    lse = (m[..., 0] + jnp.log(den)).transpose(0, 1, 3, 2)
    o = jnp.einsum("nbhqk,nbkhd->nbqhd", p, vw) / den.transpose(0, 1, 3, 2)[..., None]

    o = o.reshape(n, Lp, h, dh)[:, :L].reshape(b, dilation, L, h, dh)
    o = o.transpose(0, 2, 1, 3, 4).reshape(b, s, h, dh)
    lse = lse.reshape(n, Lp, h)[:, :L].reshape(b, dilation, L, h)
    lse = lse.transpose(0, 2, 1, 3).reshape(b, s, h)
    return o, lse

def dilated_attention_mixer(h, w_qkv, q_norm, k_norm, w_out):
    b, s, _ = h.shape
    qkv = (h @ w_qkv).reshape(b, s, N_GROUPS, 3, HEADS_PER_GROUP, HEAD_DIM)
    slopes = jnp.asarray(
        2.0 ** (-ALIBI_MAX * (np.arange(N_TOTAL_HEADS, dtype=np.float32) + 1.0) / N_TOTAL_HEADS),
        dtype=jnp.float32).reshape(N_GROUPS, HEADS_PER_GROUP)
    qn = q_norm.reshape(N_GROUPS, HEADS_PER_GROUP, HEAD_DIM)
    kn = k_norm.reshape(N_GROUPS, HEADS_PER_GROUP, HEAD_DIM)
    outs, lses = [], []
    for g, (window, dilation) in enumerate(DILATED_GROUPS):
        q = rmsnorm(qkv[:, :, g, 0], qn[g])
        k = rmsnorm(qkv[:, :, g, 1], kn[g])
        o, lse = dilated_branch(q, k, qkv[:, :, g, 2], slopes[g], window, dilation)
        outs.append(o)
        lses.append(lse)
    wts = jax.nn.softmax(jnp.stack(lses, axis=0), axis=0)
    o = jnp.sum(wts[..., None] * jnp.stack(outs, axis=0), axis=0)
    return o.astype(h.dtype).reshape(b, s, GROUP_WIDTH) @ w_out

def conv_ffn(h, w_up, dw, dw_b, w_down):
    u = causal_dwconv(h @ w_up, dw, dw_b)
    g, v = jnp.split(u, 2, axis=-1)
    return (jax.nn.silu(g) * v) @ w_down

def setup_inputs(seed: int = 0) -> dict:
    key = jax.random.key(seed)
    ks = jax.random.split(key, 24)
    f32 = jnp.float32
    nrm = lambda k, shape, scale: jax.random.normal(k, shape, f32) * scale
    D, Lc, La = D_MODEL, N_CONV_LAYERS, N_ATTN_LAYERS
    return {
        "x": jax.random.normal(ks[0], (BATCH, SEQ, D), f32),
        "norm_mix": 1.0 + nrm(ks[1], (DEPTH, D), 0.02),
        "norm_ffn": 1.0 + nrm(ks[2], (DEPTH, D), 0.02),
        "cm_w_in": nrm(ks[3], (Lc, D, CONV_EXPAND * D), D ** -0.5),
        "cm_b_in": nrm(ks[4], (Lc, CONV_EXPAND * D), 0.02),
        "cm_dw": nrm(ks[5], (Lc, CONV_KERNEL, D), CONV_KERNEL ** -0.5),
        "cm_dw_b": nrm(ks[6], (Lc, D), 0.02),
        "cm_ln_g": 1.0 + nrm(ks[7], (Lc, D), 0.02),
        "cm_ln_b": nrm(ks[8], (Lc, D), 0.02),
        "cm_w_out": nrm(ks[9], (Lc, D, D), D ** -0.5),
        "cm_b_out": nrm(ks[10], (Lc, D), 0.02),
        "at_w_qkv": nrm(ks[11], (La, D, QKV_WIDTH), D ** -0.5),
        "at_q_norm": 1.0 + nrm(ks[12], (La, N_TOTAL_HEADS, HEAD_DIM), 0.02),
        "at_k_norm": 1.0 + nrm(ks[13], (La, N_TOTAL_HEADS, HEAD_DIM), 0.02),
        "at_w_out": nrm(ks[14], (La, GROUP_WIDTH, D), GROUP_WIDTH ** -0.5),
        "ff_w_up": nrm(ks[15], (DEPTH, D, 2 * D_FF), D ** -0.5),
        "ff_dw": nrm(ks[16], (DEPTH, FFN_KERNEL, 2 * D_FF), FFN_KERNEL ** -0.5),
        "ff_dw_b": nrm(ks[17], (DEPTH, 2 * D_FF), 0.02),
        "ff_w_down": nrm(ks[18], (DEPTH, D_FF, D), D_FF ** -0.5),
    }

def reference(x, norm_mix, norm_ffn, cm_w_in, cm_b_in, cm_dw, cm_dw_b, cm_ln_g, cm_ln_b,
              cm_w_out, cm_b_out, at_w_qkv, at_q_norm, at_k_norm, at_w_out,
              ff_w_up, ff_dw, ff_dw_b, ff_w_down):
    for i in range(DEPTH):
        h = rmsnorm(x, norm_mix[i])
        j = i // N_MIXERS
        if i % N_MIXERS == 0:
            y = conformer_conv_module(h, cm_w_in[j], cm_b_in[j], cm_dw[j], cm_dw_b[j],
                                      cm_ln_g[j], cm_ln_b[j], cm_w_out[j], cm_b_out[j])
        else:
            y = dilated_attention_mixer(h, at_w_qkv[j], at_q_norm[j], at_k_norm[j], at_w_out[j])
        x = x + y
        x = x + conv_ffn(rmsnorm(x, norm_ffn[i]), ff_w_up[i], ff_dw[i], ff_dw_b[i], ff_w_down[i])
    return x


_drawn_inputs = setup_inputs


def setup_inputs(seed=0):
    import zlib

    import numpy as np

    out = dict(_drawn_inputs(seed))
    spreads = {}
    factors = {'norm_mix': 4.163,
     'norm_ffn': 4.129,
     'cm_b_in': 4.276,
     'cm_ln_g': 4.179,
     'cm_ln_b': 5.058,
     'cm_b_out': 3.004,
     'ff_dw_b': 4.381,
     'cm_dw_b': 5.21}
    for name, (base, spread) in spreads.items():
        noise = np.random.default_rng([zlib.crc32(name.encode()), seed]).standard_normal(out[name].shape)
        drawn = base * np.exp(spread * noise) if base else spread * noise
        out[name] = __import__('jax').numpy.asarray(drawn.astype(out[name].dtype))
    for name, factor in factors.items():
        out[name] = (out[name] * factor).astype(out[name].dtype)
    return out
```

```python
from contextlib import ExitStack

import concourse.bass as bass
from concourse import mybir

F32 = mybir.dt.float32
F32R = mybir.dt.float32r
ALU = mybir.AluOpType
ACT = mybir.ActivationFunctionType

P = 128
EPS = 1e-6
HI, LO = 0, 1


def conformer_ffn(nc, x, norm_mix, norm_ffn, w_in, b_in, dw, dw_b, ln_g, ln_b, w_out, b_out,
                  w_up, ff_dw, ff_dw_b, w_down, out):
    SEQ, D = x.shape
    KT = D // P
    HALF = 512
    NH = SEQ // HALF
    TH = HALF // P
    NT = SEQ // P
    TAPS = dw.shape[0]
    PAD = TAPS - 1
    FFK = ff_dw.shape[0]
    FF = w_down.shape[0]
    NP = FF // P
    NQ = NP // 2
    DH = D // 512
    assert NH == 2 and KT == 8 and DH == 2 and FFK == 3 and NP == 22

    DVE_PAIRS = [((0, 0), (0, 1)), ((1, 0), (1, 1)), ((3, 0), (4, 0)), ((6, 0), (3, 1)), ((4, 1), (6, 1))]
    POOL_UNITS = [(2, 0), (2, 1), (5, 0), (5, 1)]
    EARLY = 3
    RING = 4
    PE_TILE = KT - 1

    x_v = x.rearrange("(t p) d -> t p d", p=P)
    out_v = out.rearrange("(t p) d -> t p d", p=P)
    w_in_v = w_in.rearrange("(k p) n -> p k n", p=P)
    w_out_v = w_out.rearrange("(k p) n -> p k n", p=P)
    w_up_v = w_up.rearrange("(k p) n -> p k n", p=P)
    w_down_v = w_down.rearrange("(k p) n -> p k n", p=P)

    ctx = ExitStack()
    with ctx:
        def sb(name, shape, dt=F32):
            return ctx.enter_context(nc.sbuf_tensor(name, shape, dt))

        def sem(name):
            return ctx.enter_context(nc.semaphore(name))

        def over(base, byte, name, shape, dt=F32):
            return nc.alloc_sbuf_tensor_at(name, shape, dt, offset=base + byte)

        base = nc.sbuf_base
        base += -base % 32
        hT = sb("hT", [P, NH, 2, KT, HALF], F32R)
        w_at = base + NH * 2 * KT * HALF * 4
        wout = sb("wout", [P, 2, KT, D], F32R)
        u_all = sb("u_all", [P, NH * KT * (PAD + HALF)])
        raw = sb("raw", [P, KT * 2 * P])
        s_at = w_at + 2 * KT * D * 4 + NH * KT * (PAD + HALF) * 4 + KT * 2 * P * 4
        wsp = sb("wsp", [P, 2, 2, KT * 2 * P], F32R)
        cols = sb("cols", [P, 480])
        ident = sb("ident", [P, P])
        ones = sb("ones", [P, P])
        one_row = sb("one_row", [1, P], F32R)
        diag_acc = sb("diag_acc", [P, HALF])
        small = sb("small", [P, 32])
        dw_hi = sb("dw_hi", [P, 32], F32R)
        dw_lo = sb("dw_lo", [P, 32])
        assert s_at % 32 == 0

        x_in = over(w_at, 0, "x_in", [P, NT, D])
        rows = over(w_at, NT * D * 4, "rows", [P, 5, P])
        sig = over(w_at, NT * D * 4 + 8192, "sig", [P, NH, HALF])
        ring_early = over(w_at, NT * D * 4 + 12288, "ring_early", [P, RING, HALF])
        act = over(w_at, 0, "act", [P, 2, 2, 2, SEQ], F32R)
        wd = over(w_at, 32768, "wd", [P, 2, 2 * D], F32R)
        wd_raw = over(w_at, 49152, "wd_raw", [P, 2 * D])
        y_g = over(w_at, 57344, "y_g", [P, SEQ])
        y_v = over(w_at, 61440, "y_v", [P, SEQ])
        sq = over(s_at + 16384, 4096, "sq", [P, 2, HALF])
        std = over(s_at + 16384, 12288, "std", [P, HALF])
        ring_late = over(s_at, 0, "ring_late", [P, RING, HALF])
        hT_flat = hT[:, :, :, :, :].rearrange("p h a k s -> p h (a k s)")
        tap_diag = hT_flat[:, 0, 0:TAPS * 2 * P].rearrange("p (j a c) -> p j a c", j=TAPS, a=2)
        u_last = hT_flat[:, 1, 0:2 * NH * (PAD + HALF)].rearrange("p (a h s) -> p a h s", a=2, h=NH)
        rstd = over(s_at + 16384, 14336, "rstd", [P, HALF])

        u = [u_all[:, h * KT * (PAD + HALF):(h + 1) * KT * (PAD + HALF)].rearrange(
            "p (k s) -> p k s", k=KT) for h in range(NH)]
        u_pe = u_all[:, :].rearrange("p (h k s) -> p h k s", h=NH, k=KT)[:, :, PE_TILE, :]
        x2 = [u_all[:, h * KT * (PAD + HALF):h * KT * (PAD + HALF) + TH * D].rearrange(
            "p (t d) -> p t d", t=TH) for h in range(NH)]
        raw_pair = raw[:, :].rearrange("p (k g c) -> p k g c", k=KT, g=2)
        raw_wide = raw[:, :].rearrange("p (k c) -> p k c", k=KT)

        sig_flat = sig[:, :, :].rearrange("p h s -> p (h s)")
        sq_flat = sq[:, :, :].rearrange("p h s -> p (h s)")

        def banks(b):
            return ps[:, b:b + 2, :].rearrange("p b s -> p (b s)")

        def wtile(slot, part, k, g):
            o = (k * 2 + g) * P
            return wsp[:, slot, part, o:o + P]

        C_DW, C_FF = 0, TAPS * KT
        C_NMIX = C_FF + (FFK + 1) * 2 * NP
        C_NFFN, C_BIN, C_DWB, C_LNG, C_LNB = (C_NMIX + KT * n for n in (1, 2, 4, 5, 6))
        NCOLS = C_LNB + KT
        assert NCOLS == 480

        def col(n):
            return cols[:, n:n + 1]

        ssq, rms, rrms, eps = small[:, 0:NT], small[:, 8:16], small[:, 16:24], small[:, 24:25]

        ps = ctx.enter_context(nc.psum_tensor("ps", [P, 8, HALF], F32))
        B_G, B_A, B_CONV, B_MEAN, B_VAR, B_T, B_DOWN = 0, 2, 4, 6, 7, 4, 4

        x_loaded = [sem(f"x_loaded{t}") for t in range(NT)]
        rows_loaded, raw_loaded, wd_loaded = sem("rows_loaded"), sem("raw_loaded"), sem("wd_loaded")
        x_again = [sem(f"x_again{h}") for h in range(NH)]
        stored = sem("stored")
        ident_zero, ident_ready, ones_ready, pad_ready = (
            sem("ident_zero"), sem("ident_ready"), sem("ones_ready"), sem("pad_ready"))
        cols_turned, cols_ready = sem("cols_turned"), sem("cols_ready")
        raw_hi, raw_lo, wd_hi, wd_lo = sem("raw_hi"), sem("raw_lo"), sem("wd_hi"), sem("wd_lo")
        squared, rms_ready, rrms_ready, diag_ready = (
            sem("squared"), sem("rms_ready"), sem("rrms_ready"), sem("diag_ready"))
        turned, h_hi, h_lo = sem("turned"), sem("h_hi"), sem("h_lo")
        g_done, a_done, sig_done, glu_done = sem("g_done"), sem("a_done"), sem("sig_done"), sem("glu_done")
        tap_done = [sem("tap_done0"), sem("tap_done1")]
        prod_ready, pool_tap = sem("prod_ready"), sem("pool_tap")
        u_hi, u_lo, tap_hi, tap_lo = sem("u_hi"), sem("u_lo"), sem("tap_hi"), sem("tap_lo")
        diag_hi, diag_lo, pe_conv, pe_conv_out = (
            sem("diag_hi"), sem("diag_lo"), sem("pe_conv"), sem("pe_conv_out"))
        mean_done, centred, sq_done, var_added, std_done, rstd_done, scaled = (
            sem("mean_done"), sem("centred"), sem("sq_done"), sem("var_added"), sem("std_done"),
            sem("rstd_done"), sem("scaled"))
        z_hi, z_full, z_lo = sem("z_hi"), sem("z_full"), sem("z_lo")
        out_done, x2_done = sem("out_done"), sem("x2_done")
        upg_done, upv_done, down_done, added = sem("upg_done"), sem("upv_done"), sem("down_done"), sem("added")
        g_first, g_second, g_taps, v_first, v_second, v_taps = (
            sem("g_first"), sem("g_second"), sem("g_taps"), sem("v_first"), sem("v_second"), sem("v_taps"))
        silu_done, prod_done, act_hi, act_lo = (
            sem("silu_done"), sem("prod_done"), sem("act_hi"), sem("act_lo"))

        R_OUT = KT
        R_BOUT = R_OUT + 4
        R_UP = R_BOUT + 1
        CH = D // 4

        unit_at = {}
        for n, pair_ in enumerate(DVE_PAIRS):
            for c in range(2):
                unit_at[pair_[c]] = (tap_done[c], TAPS * (n + 1))
        for n, unit in enumerate(POOL_UNITS):
            unit_at[unit] = (pool_tap, (TAPS - 1) * (n + 1))
        for h in range(NH):
            unit_at[(PE_TILE, h)] = (pe_conv_out, h + 1)
        conv_order = [(0, 1, 2, 3, 4, 5, 7, 6), (0, 1, 2, 3, 5, 7, 4, 6)]

        block = ctx.enter_context(nc.Block())

        @block.sync
        def _(sp):
            def raw_free(n):
                sp.wait_ge(raw_lo, n)

            def load_pair(w, c, gap):
                sp.dma_start(raw_pair[:, :, 0, :], w[:, :, bass.ds(c, P)]).then_inc(raw_loaded, 16)
                sp.dma_start(raw_pair[:, :, 1, :], w[:, :, bass.ds(c + gap, P)]).then_inc(raw_loaded, 16)

            for t in range(TH):
                sp.dma_start(x_in[:, t, :], x_v[t]).then_inc(x_loaded[t], 16)
            sp.dma_start(raw_pair[:, :, 0, :], w_in_v[:, :, D:D + P]).then_inc(raw_loaded, 16)
            sp.dma_start(raw_pair[:, :, 1, :], w_in_v[:, :, 0:P]).then_inc(raw_loaded, 16)
            for t in range(TH, NT):
                sp.dma_start(x_in[:, t, :], x_v[t]).then_inc(x_loaded[t], 16)
            with sp.Fori(1, KT) as n:
                raw_free(n)
                sp.dma_start(raw_pair[:, :, 0, :], w_in_v[:, :, bass.ds(n * P + D, P)]).then_inc(raw_loaded, 16)
                sp.dma_start(raw_pair[:, :, 1, :], w_in_v[:, :, bass.ds(n * P, P)]).then_inc(raw_loaded, 16)
            for c in range(4):
                raw_free(R_OUT + c)
                for k in (0, KT // 2):
                    sp.dma_start(raw_wide[:, k:k + KT // 2, :],
                                 w_out_v[:, k:k + KT // 2, c * CH:(c + 1) * CH]).then_inc(raw_loaded, 16)
            raw_free(R_BOUT)
            for c in range(2):
                sp.dma_start(raw[0:1, c * 512:(c + 1) * 512], b_out[:, c * 512:(c + 1) * 512]).then_inc(raw_loaded, 16)
            raw_free(R_UP)
            load_pair(w_up_v, 0, FF)
            for h in range(NH):
                sp.wait_ge(z_lo, KT * (h + 1))
                sp.dma_start(x2[h], x_v[h * TH:(h + 1) * TH].rearrange("t p d -> p t d")).then_inc(x_again[h], 16)
            raw_free(R_UP + 1)
            load_pair(w_up_v, P, FF)

            def load_down(q, dst, signal):
                for k in range(2):
                    sp.dma_start(dst[:, k * D:(k + 1) * D], w_down_v[:, bass.ds(q * 2 + k, 1), :].rearrange(
                        "p k d -> p (k d)")).then_inc(signal, 16)

            sp.wait_ge(out_done, NT)
            load_down(0, wd_raw, wd_loaded)
            with sp.Fori(1, NQ - 1) as q:
                raw_free(q * 2 + R_UP)
                load_pair(w_up_v, q * (2 * P), FF)
                raw_free(q * 2 + (R_UP + 1))
                load_pair(w_up_v, q * (2 * P) + P, FF)
                sp.wait_ge(wd_lo, q)
                load_down(q, wd_raw, wd_loaded)
            for p in (NP - 2, NP - 1):
                raw_free(R_UP + p)
                load_pair(w_up_v, p * P, FF)
            raw_free(R_UP + NP)
            load_down(NQ - 1, raw, raw_loaded)
            for t in range(NT):
                sp.wait_ge(added, (NQ - 1) * NT + t + 1)
                sp.dma_start(out_v[t], x2[t // TH][:, t % TH, :]).then_inc(stored, 16)
            sp.wait_ge(stored, 16 * NT)

        @block.gpsimd
        def _(pool):
            nc.gpsimd.memset(ident[:, :], 0.0).then_inc(ident_zero, 1)
            nc.gpsimd.memset(ones[:, :], 1.0 / D).then_inc(ones_ready, 1)
            nc.gpsimd.memset(one_row[:, :].bitcast(F32), 1.0).then_inc(ones_ready, 1)
            nc.gpsimd.memset(eps, EPS).then_inc(ones_ready, 1)
            pool.wait_ge(ident_zero, 1)
            nc.gpsimd.affine_select(out=ident[:, :], in_=ident[:, :], compare_op=ALU.not_equal, fill=1.0,
                                    base=0, pattern=[[-1, P]], channel_multiplier=1).then_inc(ident_ready, 1)
            nc.gpsimd.memset(u[0][:, :, 0:PAD], 0.0).then_inc(pad_ready, 1)
            pool.wait_ge(turned, 2 * KT)
            for n, (c, h) in enumerate(POOL_UNITS):
                ring = ring_early if n < EARLY else ring_late
                for j in range(1, TAPS):
                    pool.wait_ge(prod_ready, n * TAPS + j + 1)
                    done = n * (TAPS - 1) + j - 1
                    if done:
                        pool.wait_ge(pool_tap, done)
                    before = ring[:, 0, :] if j == 1 else diag_acc[:, :]
                    dst = u[h][:, c, PAD:] if j == TAPS - 1 else diag_acc[:, :]
                    nc.gpsimd.tensor_tensor(dst, before, ring[:, j % RING, :], ALU.add).then_inc(pool_tap, 1)

        @block.scalar
        def _(a):
            dwr = dw.rearrange("j (t c) -> (j t) c", c=P)
            ffr = ff_dw.rearrange("j (t c) -> (j t) c", c=P)
            ffb = ff_dw_b.rearrange("o (t c) -> (o t) c", c=P)
            n_dma = 0
            R1, R2 = P, TAPS * KT - P
            for dst, src in ((rows[0:R1, 0, :], dwr[0:R1]), (rows[0:R2, 1, :], dwr[R1:R1 + R2]),
                             (rows[0:4 * NP, 2, :], ffr[0:4 * NP]), (rows[0:2 * NP, 3, :], ffr[4 * NP:6 * NP]),
                             (rows[2 * NP:4 * NP, 3, :], ffb)):
                a.dma_start(dst, src).then_inc(rows_loaded, 16)
                n_dma += 1
            r = 0
            for v in (norm_mix, norm_ffn, b_in, dw_b, ln_g, ln_b):
                k = v.shape[1] // P
                a.dma_start(rows[r:r + k, 4, :], v.rearrange("o (t c) -> (o t) c", c=P)).then_inc(rows_loaded, 16)
                r += k
                n_dma += 1
            assert n_dma == 11

            def split_hi(n, dst, src):
                a.wait_ge(raw_loaded, 32 * (n + 1))
                nc.scalar.activation(dst, src, ACT.Copy).then_inc(raw_hi, 1)

            def squares(n_before, t, src, junk, waits):
                for s, v in waits:
                    a.wait_ge(s, v)
                if n_before:
                    a.wait_ge(squared, n_before)
                nc.scalar.activation(junk, src, ACT.Square, accum_out=ssq[:, t:t + 1]).then_inc(squared, 1)

            def root(h, n):
                a.wait_ge(squared, n)
                nc.scalar.activation(rms[:, h * TH:(h + 1) * TH], ssq[:, h * TH:(h + 1) * TH], ACT.Sqrt,
                                     bias=eps, scale=1.0 / D).then_inc(rms_ready, 1)

            def turned_hi(h, stage, gain):
                for k in range(KT):
                    n = (2 * stage + h) * KT + k
                    a.wait_ge(turned, n + 1)
                    nc.scalar.activation(hT[:, h, HI, k, :], ps[:, B_T + n % 4, :], ACT.Copy,
                                         scale=col(gain + k)).then_inc(h_hi, 1)

            a.wait_ge(ones_ready, 3)
            a.wait_ge(pad_ready, 1)
            for t in range(TH):
                squares(t, t, x_in[:, t, :], sig_flat, [(x_loaded[t], 16)])
            root(0, TH)
            split_hi(0, wsp[:, 0, HI, :], raw[:, :])
            a.wait_ge(cols_ready, 1)
            turned_hi(0, 0, C_NMIX)
            for t in range(TH, NT):
                squares(t, t, x_in[:, t, :], sig_flat, [(x_loaded[t], 16)])
            root(1, NT)
            turned_hi(1, 0, C_NMIX)

            def sigmoids(c, last):
                for h in range(NH):
                    a.wait_ge(g_done, c * NH + h + 1)
                    if last is not None:
                        a.wait_ge(glu_done, last + h)
                    nc.scalar.activation(sig[:, h, :], ps[:, B_G + h, :], ACT.Sigmoid,
                                         bias=cols[:, bass.ds(c + (C_BIN + KT), 1)]).then_inc(sig_done, 1)

            product_at = [0]

            def products(count):
                for i in range(product_at[0], product_at[0] + count):
                    n, j = divmod(i, TAPS)
                    c, h = POOL_UNITS[n]
                    ring = ring_early if n < EARLY else ring_late
                    if j == 0:
                        a.wait_ge(glu_done, NH * c + h + 1)
                    before = j - RING if j >= RING else (None if n in (0, EARLY) else TAPS - 1 - (TAPS - 1 - j) % RING - TAPS)
                    if before is not None:
                        at = n if before >= 0 else n - 1
                        tap = before % TAPS
                        a.wait_ge(pool_tap, at * (TAPS - 1) + max(tap, 1))
                    src, w = u[h][:, c, j:j + HALF], col(C_DW + j * KT + c)
                    if j == 0:
                        ins = nc.scalar.activation(ring[:, 0, :], src, ACT.Identity, scale=w, bias=col(C_DWB + c))
                    else:
                        ins = nc.scalar.activation(ring[:, j % RING, :], src, ACT.Copy, scale=w)
                    ins.then_inc(prod_ready, 1)
                product_at[0] += count

            split_hi(1, wsp[:, 1, HI, :], raw[:, :])
            a.wait_ge(squared, NT)
            sigmoids(0, None)
            for c in range(1, KT):
                if c + 1 < KT:
                    a.wait_ge(a_done, c * NH)
                    split_hi(c + 1, wsp[:, (c + 1) % 2, HI, :], raw[:, :])
                sigmoids(c, (c - 1) * NH + 1)
                if c >= POOL_UNITS[0][0] and c < KT - 1:
                    products(16)

            a.wait_ge(glu_done, KT * NH)
            a.wait_ge(a_done, KT * NH)
            nc.scalar.activation(u_last[:, HI, :, :], u_pe, ACT.Copy).then_inc(u_hi, 1)
            products(EARLY * TAPS - product_at[0])
            a.wait_ge(tap_lo, 1)
            for j in range(TAPS):
                nc.scalar.activation(tap_diag[:, j, HI, :], ident[:, :], ACT.Copy,
                                     scale=col(C_DW + j * KT + PE_TILE)).then_inc(diag_hi, 1)
                nc.scalar.activation(tap_diag[:, j, LO, :], ident[:, :], ACT.Copy,
                                     scale=dw_lo[:, j:j + 1]).then_inc(diag_lo, 1)
                products(1)
                if j % 7 == 6:
                    a.wait_ge(pool_tap, EARLY * (TAPS - 1))
                    c = j // 7
                    split_hi(R_OUT + c, wout[:, HI, :, c * CH:(c + 1) * CH], raw_wide)
            a.wait_ge(pe_conv, 1)
            for h in range(NH):
                nc.scalar.activation(u[h][:, PE_TILE, PAD:], ps[:, h, :], ACT.Identity,
                                     bias=col(C_DWB + PE_TILE)).then_inc(pe_conv_out, 1)
            split_hi(R_BOUT, wsp[0:1, 1, HI, 0:D], raw[0:1, 0:D])
            def layernorm(h):
                for k in range(KT):
                    n = h * KT + k
                    a.wait_ge(centred, n + 1)
                    if n >= 2:
                        a.wait_ge(var_added, n - 1)
                    nc.scalar.activation(sq[:, n % 2, :], u[h][:, conv_order[h][k], PAD:], ACT.Square).then_inc(sq_done, 1)
                a.wait_ge(var_added, (h + 1) * KT)
                if h:
                    a.wait_ge(rstd_done, h)
                nc.scalar.activation(std[:, :], ps[:, B_VAR, :], ACT.Sqrt, bias=eps).then_inc(std_done, 1)
                if h:
                    a.wait_ge(out_done, TH)
                def silu(k, dst, signal):
                    nc.scalar.activation(dst, u[h][:, k, PAD:], ACT.Silu, scale=col(C_LNG + k),
                                         bias=col(C_LNB + k)).then_inc(signal, 1)

                for k in range(KT + 1):
                    if k < KT:
                        a.wait_ge(scaled, h * KT + k + 1)
                        silu(k, hT[:, 1, HI, k, :], z_hi)
                    if k:
                        a.wait_ge(z_hi, h * KT + k)
                        silu(k - 1, u[h][:, k - 1, PAD:], z_full)

            layernorm(0)
            a.wait_ge(pool_tap, (TAPS - 1) * len(POOL_UNITS))
            split_hi(R_UP, wsp[:, 0, HI, :], raw[:, :])
            layernorm(1)
            for h in range(NH):
                for t in range(h * TH, (h + 1) * TH):
                    squares(NT + t, t, x2[h][:, t % TH, :], sq_flat, [(x2_done, t + 1), (var_added, 2 * KT)])
                root(h, NT + (h + 1) * TH)
            for h in range(NH):
                turned_hi(h, 1, C_NFFN)

            def first_tap(p, g, bank, done, dst, s, dst_free):
                for w, v in dst_free:
                    a.wait_ge(w, v)
                a.wait_ge(done, p + 1)
                f = p + g * NP
                nc.scalar.activation(dst[:, :], ps[:, bank:bank + 2, :], ACT.Identity,
                                     scale=cols[:, bass.ds(f + (C_FF + 2 * 2 * NP), 1)],
                                     bias=cols[:, bass.ds(f + (C_FF + 3 * 2 * NP), 1)]).then_inc(s, 1)

            def split_up(p, slot):
                a.wait_ge(raw_loaded, (p + (R_UP + 1)) * 32)
                nc.scalar.activation(wsp[:, slot, HI, :], raw[:, :], ACT.Copy).then_inc(raw_hi, 1)

            def pair(p, par, slot, first=False, wd_of=None):
                first_tap(p, 0, B_G, upg_done, y_g, g_first, [] if first else [(prod_done, p)])
                split_up(p + 1, 1 - par)
                if wd_of is not None:
                    a.wait_ge(wd_loaded, (wd_of + 1) * 32)
                    nc.scalar.activation(wd[:, HI, :], wd_raw[:, :], ACT.Copy).then_inc(wd_hi, 1)
                first_tap(p, 1, B_A, upv_done, y_v, v_first, [] if first else [(act_lo, p)])
                a.wait_ge(g_taps, p + 1)
                nc.scalar.activation(y_g[:, :], y_g[:, :], ACT.Silu).then_inc(silu_done, 1)
                a.wait_ge(prod_done, p + 1)
                nc.scalar.activation(act[:, slot, par, HI, :], y_v[:, :], ACT.Copy).then_inc(act_hi, 1)

            pair(0, 0, 0, first=True)
            pair(1, 1, 0)
            with a.Fori(0, (NQ - 1) // 2) as i:
                for s in range(2):
                    p = i * 4 + 2 * (s + 1)
                    pair(p, 0, (s + 1) % 2, wd_of=i * 2 + s)
                    pair(p + 1, 1, (s + 1) % 2)

        @block.vector
        def _(dve):
            v = nc.vector

            def split_lo(n, lo, src, hi):
                dve.wait_ge(raw_hi, n + 1)
                v.tensor_tensor(lo, src, hi.bitcast(F32), ALU.subtract).then_inc(raw_lo, 1)

            def split_pair(n, slot):
                split_lo(n, wsp[:, slot, LO, :], raw[:, :], wsp[:, slot, HI, :])

            def diagonals(stage, h, waits):
                n = 2 * stage + h + 1
                dve.wait_ge(rms_ready, n)
                v.reciprocal(rrms[:, h * TH:(h + 1) * TH], rms[:, h * TH:(h + 1) * TH]).then_inc(rrms_ready, 1)
                for w, value in waits:
                    dve.wait_ge(w, value)
                dve.wait_ge(rrms_ready, n)
                for t in range(TH):
                    ins = v.tensor_scalar(diag_acc[:, t * P:(t + 1) * P], ident[:, :],
                                          rrms[:, h * TH + t:h * TH + t + 1], None, ALU.mult)
                ins.then_inc(diag_ready, 1)

            def turned_lo(stage, h, gain):
                for k in range(KT):
                    n = (2 * stage + h) * KT + k
                    dve.wait_ge(h_hi, n + 1)
                    v.scalar_tensor_tensor(out=hT[:, h, LO, k, :], in0=ps[:, B_T + n % 4, :], scalar=col(gain + k),
                                           in1=hT[:, h, HI, k, :].bitcast(F32), op0=ALU.mult,
                                           op1=ALU.subtract).then_inc(h_lo, 1)

            def glu(c):
                for h in range(NH):
                    dve.wait_ge(sig_done, c * NH + h + 1)
                    dve.wait_ge(a_done, c * NH + h + 1)
                    spots = [(u[h][:, c, PAD:], 0)]
                    if h == 0:
                        spots.insert(0, (u[1][:, c, 0:PAD], HALF - PAD))
                    for dst, s in spots:
                        ins = v.scalar_tensor_tensor(out=dst, in0=ps[:, B_A + h, s:], scalar=col(C_BIN + c),
                                                     in1=sig[:, h, s:], op0=ALU.add, op1=ALU.mult)
                    ins.then_inc(glu_done, 1)

            def conv_pair(n, hooks):
                for j in range(TAPS):
                    for i, (c, h) in enumerate(DVE_PAIRS[n]):
                        if n or j:
                            dve.wait_ge(tap_done[i], n * TAPS + j)
                        acc = ps[:, B_CONV + i, :]
                        src, w = u[h][:, c, j:j + HALF], col(C_DW + j * KT + c)
                        if j == 0:
                            ins = v.tensor_scalar(acc, src, w, col(C_DWB + c), ALU.mult, ALU.add)
                        else:
                            ins = v.scalar_tensor_tensor(out=src if j == TAPS - 1 else acc, in0=src, scalar=w,
                                                         in1=acc, op0=ALU.mult, op1=ALU.add)
                        ins.then_inc(tap_done[i], 1)
                    for work in hooks.get(j, ()):
                        work()

            def centre(h):
                dve.wait_ge(mean_done, h + 1)
                for c in conv_order[h]:
                    v.tensor_tensor(u[h][:, c, PAD:], u[h][:, c, PAD:], ps[:, B_MEAN, :],
                                    ALU.subtract).then_inc(centred, 1)

            def scale(h):
                dve.wait_ge(std_done, h + 1)
                v.reciprocal(rstd[:, :], std[:, :]).then_inc(rstd_done, 1)
                dve.wait_ge(rstd_done, h + 1)
                for k in range(KT):
                    v.tensor_tensor(u[h][:, k, PAD:], u[h][:, k, PAD:], rstd[:, :], ALU.mult).then_inc(scaled, 1)

            def z_low(h):
                for k in range(KT):
                    dve.wait_ge(z_full, h * KT + k + 1)
                    v.tensor_tensor(hT[:, 1, LO, k, :], u[h][:, k, PAD:], hT[:, 1, HI, k, :].bitcast(F32),
                                    ALU.subtract).then_inc(z_lo, 1)

            def add_out(t):
                dve.wait_ge(out_done, t + 1)
                dve.wait_ge(x_again[t // TH], 16)
                x2_t = x2[t // TH][:, t % TH, :]
                v.tensor_tensor(x2_t, x2_t, banks(2 * (t % 2)), ALU.add).then_inc(x2_done, 1)

            def quarter(c):
                split_lo(R_OUT + c, wout[:, LO, :, c * CH:(c + 1) * CH], raw_wide, wout[:, HI, :, c * CH:(c + 1) * CH])

            dve.wait_ge(cols_turned, 1)
            v.tensor_copy(cols[:, :], ps[:, 0, 0:NCOLS]).then_inc(cols_ready, 1)
            dve.wait_ge(ident_ready, 1)
            diagonals(0, 0, [(cols_ready, 1)])
            split_pair(0, 0)
            turned_lo(0, 0, C_NMIX)
            diagonals(0, 1, [(turned, KT)])
            turned_lo(0, 1, C_NMIX)
            split_pair(1, 1)
            glu(0)
            taps_pe = cols[:, C_DW + PE_TILE:C_DW + TAPS * KT:KT]
            v.tensor_copy(dw_hi[:, 0:TAPS], taps_pe).then_inc(tap_hi, 1)
            dve.wait_ge(tap_hi, 1)
            v.tensor_tensor(dw_lo[:, 0:TAPS], taps_pe, dw_hi[:, 0:TAPS].bitcast(F32), ALU.subtract).then_inc(tap_lo, 1)

            def last_tile_lo():
                dve.wait_ge(u_hi, 1)
                v.tensor_tensor(u_last[:, LO, :, :], u_pe, u_last[:, HI, :, :].bitcast(F32), ALU.subtract).then_inc(u_lo, 1)

            dve.wait_ge(pad_ready, 1)
            conv_pair(0, {4: [lambda: split_pair(2, 0)], 16: [lambda: glu(1)], 25: [lambda: split_pair(3, 1)]})
            glu(2)
            conv_pair(1, {4: [lambda: split_pair(4, 0)], 13: [lambda: glu(3)],
                          20: [lambda: split_pair(5, 1)], 28: [lambda: glu(4)]})
            conv_pair(2, {3: [lambda: split_pair(6, 0)], 11: [lambda: glu(5)],
                          16: [lambda: split_pair(7, 1)], 26: [lambda: glu(6)]})
            conv_pair(3, {7: [lambda: glu(7), last_tile_lo], 16: [lambda: quarter(0)], 23: [lambda: quarter(1)],
                          29: [lambda: quarter(2)]})
            quarter(3)
            split_lo(R_BOUT, wsp[0:1, 1, LO, 0:D], raw[0:1, 0:D], wsp[0:1, 1, HI, 0:D])
            centre(0)
            scale(0)
            z_low(0)
            conv_pair(4, {4: [lambda: split_pair(R_UP, 0)], 9: [lambda: add_out(0)], 18: [lambda: add_out(1)],
                          26: [lambda: add_out(2)]})
            add_out(3)
            centre(1)
            scale(1)
            dve.wait_ge(out_done, TH)
            z_low(1)
            add_out(4)
            add_out(5)
            diagonals(1, 0, [(pool_tap, (TAPS - 1) * len(POOL_UNITS))])
            add_out(6)
            add_out(7)
            turned_lo(1, 0, C_NFFN)
            diagonals(1, 1, [(turned, 3 * KT)])
            turned_lo(1, 1, C_NFFN)

            def later_taps(p, g, bank, y, first, second, done):
                src = banks(bank)
                f = p + g * NP
                dve.wait_ge(first, p + 1)
                v.scalar_tensor_tensor(out=y[:, 1:], in0=src[:, 0:SEQ - 1],
                                       scalar=cols[:, bass.ds(f + (C_FF + 2 * NP), 1)], in1=y[:, 1:],
                                       op0=ALU.mult, op1=ALU.add).then_inc(second, 1)
                dve.wait_ge(second, p + 1)
                v.scalar_tensor_tensor(out=y[:, 2:], in0=src[:, 0:SEQ - 2],
                                       scalar=cols[:, bass.ds(f + C_FF, 1)], in1=y[:, 2:],
                                       op0=ALU.mult, op1=ALU.add).then_inc(done, 1)

            def add_down(n, t):
                dve.wait_ge(down_done, n + 1)
                x2_t = x2[t // TH][:, t % TH, :]
                v.tensor_tensor(x2_t, x2_t, banks(B_DOWN + 2 * (t % 2)), ALU.add).then_inc(added, 1)

            def pair(p, par, slot, wd_of=None, down_of=None):
                adds = [] if down_of is None else list(range(NT))

                def add():
                    if adds:
                        t = adds.pop(0)
                        add_down(down_of * NT + t, t)

                later_taps(p, 0, B_G, y_g, g_first, g_second, g_taps)
                dve.wait_ge(raw_hi, p + (R_UP + 2))
                v.tensor_tensor(wsp[:, 1 - par, LO, :], raw[:, :], wsp[:, 1 - par, HI, :].bitcast(F32),
                                ALU.subtract).then_inc(raw_lo, 1)
                if wd_of is not None:
                    dve.wait_ge(wd_hi, wd_of + 1)
                    v.tensor_tensor(wd[:, LO, :], wd_raw[:, :], wd[:, HI, :].bitcast(F32),
                                    ALU.subtract).then_inc(wd_lo, 1)
                later_taps(p, 1, B_A, y_v, v_first, v_second, v_taps)
                add()
                dve.wait_ge(silu_done, p + 1)
                dve.wait_ge(v_taps, p + 1)
                v.tensor_tensor(y_v[:, :], y_g[:, :], y_v[:, :], ALU.mult).then_inc(prod_done, 1)
                add()
                dve.wait_ge(act_hi, p + 1)
                v.tensor_tensor(act[:, slot, par, LO, :], y_v[:, :], act[:, slot, par, HI, :].bitcast(F32),
                                ALU.subtract).then_inc(act_lo, 1)
                while adds:
                    add()

            pair(0, 0, 0)
            pair(1, 1, 0)
            with dve.Fori(0, (NQ - 1) // 2) as i:
                for s in range(2):
                    p = i * 4 + 2 * (s + 1)
                    pair(p, 0, (s + 1) % 2, wd_of=i * 2 + s)
                    pair(p + 1, 1, (s + 1) % 2, down_of=i * 2 + s)
            for t in range(NT):
                add_down((NQ - 1) * NT + t, t)

        @block.tensor
        def _(pe):
            mm = nc.tensor.matmul
            PASSES = ((HI, HI), (HI, LO), (LO, HI))

            def turn(stage, h, src):
                pe.wait_ge(diag_ready, 2 * stage + h + 1)
                for k in range(KT):
                    n = (2 * stage + h) * KT + k
                    if n >= 4:
                        pe.wait_ge(h_lo, n - 3)
                    for t in range(TH):
                        ins = mm(ps[:, B_T + n % 4, t * P:(t + 1) * P], src[:, t, k * P:(k + 1) * P],
                                 diag_acc[:, t * P:(t + 1) * P], start=True, stop=True)
                    ins.then_inc(turned, 1)

            def project(bank, slot, g, h, signal, each=None):
                for k in range(KT):
                    if each is not None:
                        pe.wait_ge(h_lo, each + k + 1)
                    for n, (pw, px) in enumerate(PASSES):
                        ins = mm(ps[:, bank, :], wtile(slot, pw, k, g), hT[:, h, px, k, :],
                                 start=(k == 0 and n == 0), stop=(k == KT - 1 and n == 2))
                if signal is not None:
                    ins.then_inc(signal, 1)

            def in_pair(c, slot):
                pe.wait_ge(raw_lo, c + 1)
                for bank, g, free, signal in ((B_G, 0, sig_done, g_done), (B_A, 1, glu_done, a_done)):
                    for h in range(NH):
                        pe.wait_ge(free, (c - 1) * NH + h + 1)
                        project(bank + h, slot, g, h, signal)

            pe.wait_ge(ident_ready, 1)
            pe.wait_ge(rows_loaded, 11 * 16)
            at = 0
            for r, k in enumerate((P, TAPS * KT - P, 4 * NP, 4 * NP, 7 * KT)):
                ins = nc.tensor.transpose(ps[:, 0, at:at + k], rows[0:k, r, :], ident[0:k, 0:k])
                at += k
            assert at == NCOLS
            ins.then_inc(cols_turned, 1)

            pe.wait_ge(ones_ready, 3)
            for h in range(NH):
                turn(0, h, x_in[:, h * TH:(h + 1) * TH, :])
                pe.wait_ge(cols_ready, 1)
                pe.wait_ge(raw_lo, 1)
                project(B_G + h, 0, 0, h, g_done, each=h * KT)
                project(B_A + h, 0, 1, h, a_done)
            with pe.Fori(1, KT - 1, 2) as c:
                in_pair(c, 1)
                in_pair(c + 1, 0)
            in_pair(KT - 1, 1)

            def mean(h):
                if h:
                    pe.wait_ge(centred, h * KT)
                for n, c in enumerate(conv_order[h]):
                    s, value = unit_at[(c, h)]
                    pe.wait_ge(s, value)
                    ins = mm(ps[:, B_MEAN, :], ones[:, :], u[h][:, c, PAD:], start=(n == 0), stop=(n == KT - 1))
                ins.then_inc(mean_done, 1)

            def variance(h):
                if h:
                    pe.wait_ge(std_done, h)
                for k in range(KT):
                    n = h * KT + k
                    pe.wait_ge(sq_done, n + 1)
                    mm(ps[:, B_VAR, :], ones[:, :], sq[:, n % 2, :], start=(k == 0),
                       stop=(k == KT - 1)).then_inc(var_added, 1)

            def project_out(t):
                h = t // TH
                if t % TH == 0:
                    pe.wait_ge(raw_lo, R_BOUT + 1)
                    pe.wait_ge(z_lo, (h + 1) * KT)
                if t >= 2:
                    pe.wait_ge(x2_done, t - 1)
                for b in range(DH):
                    bank, d = 2 * (t % 2) + b, slice(b * 512, (b + 1) * 512)
                    for part in (HI, LO):
                        mm(ps[:, bank, :], one_row[:, :], wsp[0:1, 1, part, d], start=(part == HI), stop=False)
                    for k in range(KT):
                        for n, (pz, pw) in enumerate(PASSES):
                            ins = mm(ps[:, bank, :], hT[:, 1, pz, k, (t % TH) * P:(t % TH + 1) * P],
                                     wout[:, pw, k, d], start=False, stop=(k == KT - 1 and n == 2))
                ins.then_inc(out_done, 1)

            pe.wait_ge(u_lo, 1)
            for j in range(TAPS):
                pe.wait_ge(diag_hi, j + 1)
                pe.wait_ge(diag_lo, j + 1)
                for h in range(NH):
                    for n, (pt, pu) in enumerate(PASSES):
                        ins = mm(ps[:, h, :], tap_diag[:, j, pt, :], u_last[:, pu, h, j:j + HALF],
                                 start=(j == 0 and n == 0), stop=(j == TAPS - 1 and n == 2))
            ins.then_inc(pe_conv, 1)

            mean(0)
            variance(0)
            pe.wait_ge(pe_conv_out, NH)
            for t in range(TH):
                project_out(t)
            mean(1)
            variance(1)
            for t in range(TH, NT):
                project_out(t)

            def down(q, slot, weights):
                pe.wait_ge(act_lo, q * 2 + 2)
                for t in range(NT):
                    if t >= 2:
                        pe.wait_ge(added, q * NT + (t - 1))
                    for b in range(DH):
                        for k in range(2):
                            for n, (pa, pw) in enumerate(PASSES):
                                o = k * D + b * 512
                                ins = mm(ps[:, B_DOWN + 2 * (t % 2) + b, :], act[:, slot, k, pa, t * P:(t + 1) * P],
                                         weights(pw, o), start=(k == 0 and n == 0), stop=(k == 1 and n == 2))
                    ins.then_inc(down_done, 1)

            def up_pair(p, slot):
                pe.wait_ge(raw_lo, p + (R_UP + 1))
                for bank, g, free, signal in ((B_G, 0, g_taps, upg_done), (B_A, 1, v_taps, upv_done)):
                    pe.wait_ge(free, p)
                    project(bank, slot, g, 0, None)
                    project(bank + 1, slot, g, 1, signal)

            for h in range(NH):
                turn(1, h, x2[h])
                pe.wait_ge(x2_done, NT)
                pe.wait_ge(raw_lo, R_UP + 1)
                project(B_G + h, 0, 0, h, upg_done if h else None, each=(2 + h) * KT)
                project(B_A + h, 0, 1, h, upv_done if h else None)
            up_pair(1, 1)
            with pe.Fori(0, (NQ - 1) // 2) as i:
                for s in range(2):
                    p = i * 4 + 2 * (s + 1)
                    up_pair(p, 0)
                    up_pair(p + 1, 1)
                    q = i * 2 + s
                    pe.wait_ge(wd_lo, q + 1)
                    down(q, s % 2, lambda part, o: wd[:, part, o:o + 512])
            pe.wait_ge(raw_lo, R_UP + NP + 1)
            pe.wait_ge(added, (NQ - 1) * NT)
            down(NQ - 1, 0, lambda part, o: wsp[:, 0, part, o:o + 512])


_INS = ["x", "norm_mix", "norm_ffn", "cm_w_in", "cm_b_in", "cm_dw", "cm_dw_b", "cm_ln_g", "cm_ln_b",
        "cm_w_out", "cm_b_out", "ff_w_up", "ff_dw", "ff_dw_b", "ff_w_down"]


def kernel(**inputs):
    import numpy as np
    import concourse.bacc as bacc
    from concourse.bass_utils import run_bass_kernel_spmd

    nc = bacc.Bacc("TRN2", target_bir_lowering=False, num_devices=1)
    arrays, args = {}, []
    for name in _INS:
        a = np.ascontiguousarray(inputs[name])
        arrays[f"in_{name}"] = a
        ap = nc.dram_tensor(f"in_{name}", a.shape, mybir.dt.from_np(a.dtype), kind="ExternalInput").ap()
        args.append(ap if len(a.shape) == 2 else ap.rearrange("o a b -> (o a) b"))
    shape = inputs["x"].shape
    out = nc.dram_tensor("out", shape, F32, kind="ExternalOutput").ap()
    conformer_ffn(nc, *args, out.rearrange("o a b -> (o a) b"))
    r = run_bass_kernel_spmd(nc, [arrays], core_ids=[0])
    return r.results[0]["out"]
```

```python
from contextlib import ExitStack

import concourse.bass as bass
from concourse import mybir

F32 = mybir.dt.float32
F32R = mybir.dt.float32r
ALU = mybir.AluOpType
ACT = mybir.ActivationFunctionType

P = 128
EPS = 1e-6
HI, LO = 0, 1


def conformer_ffn(nc, x, norm_mix, norm_ffn, w_in, b_in, dw, dw_b, ln_g, ln_b, w_out, b_out,
                  w_up, ff_dw, ff_dw_b, w_down, out):
    SEQ, D = x.shape
    KT = D // P
    HALF = 512
    NH = SEQ // HALF
    TH = HALF // P
    NT = SEQ // P
    TAPS = dw.shape[0]
    PAD = TAPS - 1
    FFK = ff_dw.shape[0]
    FF = w_down.shape[0]
    NP = FF // P
    NQ = NP // 2
    DH = D // 512
    assert NH == 2 and KT == 8 and DH == 2 and FFK == 3 and NP == 22

    CHAINS = [((0, 0),), ((2, 0),), ((3, 0), (4, 0)), ((6, 0), (7, 0)), ((0, 1), (1, 1))]
    POOL_UNITS = [(1, 0), (5, 0), (2, 1), (3, 1)]
    LOOP_FIRST = 4
    RING = 3
    TAPS_BEFORE, TAPS_A_TURN = 3, 6
    assert TAPS_BEFORE % RING == 0 and TAPS_A_TURN % RING == 0
    NI = (NQ - 3) // 2

    x_v = x.rearrange("(t p) d -> t p d", p=P)
    out_v = out.rearrange("(t p) d -> t p d", p=P)
    w_in_v = w_in.rearrange("(k p) n -> p k n", p=P)
    w_out_v = w_out.rearrange("(k p) n -> p k n", p=P)
    w_up_v = w_up.rearrange("(k p) n -> p k n", p=P)
    w_down_v = w_down.rearrange("(k p) n -> p k n", p=P)

    ctx = ExitStack()
    with ctx:
        def sb(name, shape, dt=F32):
            return ctx.enter_context(nc.sbuf_tensor(name, shape, dt))

        def sem(name):
            return ctx.enter_context(nc.semaphore(name))

        ITEM = KT * 2 * P
        W = PAD + HALF
        work_at = nc.sbuf_base + -nc.sbuf_base % 32
        work = sb("work", [P, 14336])
        hT = sb("hT", [P, NH, 2, KT, HALF], F32R)
        u_all = sb("u_all", [P, NH * KT * W])
        raw = sb("raw", [P, 2, ITEM])
        wsp = sb("wsp", [P, 2, 2, ITEM], F32R)
        cols = sb("cols", [P, 480])
        ident = sb("ident", [P, P])
        ones = sb("ones", [P, P])
        one_row = sb("one_row", [1, P], F32R)
        acc_sum = sb("acc_sum", [P, HALF])
        small = sb("small", [P, 32])
        tails = sb("tails", [P, 2 * NP * (FFK - 1)])

        def over(byte, name, shape, dt=F32):
            size = 4
            for n in shape[1:]:
                size *= n
            assert byte + size <= 14336 * 4
            return nc.alloc_sbuf_tensor_at(name, shape, dt, offset=work_at + byte)

        x_in = over(0, "x_in", [P, NT, D])
        rows = over(32768, "rows", [P, 5, P])
        sig = over(53248, "sig", [P, NH, HALF])
        diag = over(32768, "diag", [P, HALF])
        act = over(0, "act", [P, 2, 2, 2, HALF], F32R)
        wd = over(16384, "wd", [P, 2, ITEM], F32R)
        y_g = over(32768, "y_g", [P, HALF])
        y_v = over(34816, "y_v", [P, HALF])
        ring = over(36864, "ring", [P, RING, HALF])
        norm = [over(at, f"norm{h}", [P, 4, HALF]) for h, at in enumerate((0, 36864))]
        b_row = over(45056, "b_row", [1, 2, D], F32R)

        u = [u_all[:, h * KT * W:(h + 1) * KT * W].rearrange("p (k s) -> p k s", k=KT) for h in range(NH)]
        x2 = [u_all[:, h * KT * W:h * KT * W + TH * D].rearrange("p (t d) -> p t d", t=TH) for h in range(NH)]
        sig_flat = sig[:, :, :].rearrange("p h s -> p (h s)")
        junk = [norm[h][:, 0:2, :].rearrange("p n s -> p (n s)") for h in range(NH)]

        def banks(b):
            return ps[:, b:b + 2, :].rearrange("p b s -> p (b s)")

        def raw_pair(n):
            return raw[:, n % 2, :].rearrange("p (k g c) -> p k g c", k=KT, g=2)

        def wtile(slot, part, k, g):
            o = (k * 2 + g) * P
            return wsp[:, slot, part, o:o + P]

        C_DW, C_FF = 0, TAPS * KT
        C_NMIX = C_FF + (FFK + 1) * 2 * NP
        C_NFFN, C_BIN, C_DWB, C_LNG, C_LNB = (C_NMIX + KT * n for n in (1, 2, 4, 5, 6))
        NCOLS = C_LNB + KT
        assert NCOLS == 480

        def col(n):
            return cols[:, n:n + 1]

        ssq, rms, rrms, eps = small[:, 0:NT], small[:, 8:16], small[:, 16:24], small[:, 24:25]

        ps = ctx.enter_context(nc.psum_tensor("ps", [P, 8, HALF], F32))
        B_G, B_A, B_CONV, B_T, B_DOWN = 0, 2, 4, 4, 4
        B_MEAN, B_VAR = (6, 3), (7, 2)
        B_UPG, B_UPV, B_LOOP = 0, 1, 2

        x_loaded = [sem(f"x_loaded{t}") for t in range(NT)]
        rows_loaded = sem("rows_loaded")
        raw_loaded = [sem(f"raw_loaded{b}") for b in range(2)]
        x_again = [sem(f"x_again{h}") for h in range(NH)]
        stored = sem("stored")
        ident_zero, ident_ready, ones_ready, pad_ready = (
            sem("ident_zero"), sem("ident_ready"), sem("ones_ready"), sem("pad_ready"))
        cols_turned, cols_ready = sem("cols_turned"), sem("cols_ready")
        raw_hi, raw_lo = sem("raw_hi"), sem("raw_lo")
        squared, rms_ready, rrms_ready, diag_ready = (
            sem("squared"), sem("rms_ready"), sem("rrms_ready"), sem("diag_ready"))
        turned, h_hi, h_lo = sem("turned"), sem("h_hi"), sem("h_lo")
        g_done, a_done, sig_done, glu_done = sem("g_done"), sem("a_done"), sem("sig_done"), sem("glu_done")
        tap_done = [sem("tap_done0"), sem("tap_done1")]
        conv_joined, prod_ready, pool_tap = sem("conv_joined"), sem("prod_ready"), sem("pool_tap")
        mean_done, centred, sq_done, var_added, std_done, rstd_done, scaled = (
            sem("mean_done"), sem("centred"), sem("sq_done"), sem("var_added"), sem("std_done"),
            sem("rstd_done"), sem("scaled"))
        z_hi, z_full, z_lo = sem("z_hi"), sem("z_full"), sem("z_lo")
        out_read, out_done, x2_done = sem("out_read"), sem("out_done"), sem("x2_done")
        upg_done, upv_done, down_done, added = sem("upg_done"), sem("upv_done"), sem("down_done"), sem("added")
        g_first, g_second, g_taps, v_first, v_second, v_taps = (
            sem("g_first"), sem("g_second"), sem("g_taps"), sem("v_first"), sem("v_second"), sem("v_taps"))
        silu_done, prod_done, act_hi, act_lo = (
            sem("silu_done"), sem("prod_done"), sem("act_hi"), sem("act_lo"))

        I_BOUT = 2 * KT - 1
        I_OUT = (tuple(range(I_BOUT + 1, I_BOUT + 5)), )
        I_IN_LAST = I_BOUT + 5
        F0 = I_IN_LAST + 1
        last0 = F0 + 2 + 3 * (NQ - 1)
        I_OUT += ((last0, last0 + 1, last0 + 3, last0 + 4), )
        I_DOWN_LAST = last0 + 2
        F1 = last0 + 5
        I_FFN = (F0, F1)
        I_END = F1 + 2 + 3 * (NQ - 1)

        def item_ready(eng, n):
            eng.wait_ge(raw_loaded[n % 2], (n // 2 + 1) * 32)

        unit_at, taps_at, n_joined = {}, [0, 0], 0
        for units in CHAINS:
            if len(units) == 2:
                for i in range(2):
                    taps_at[i] += TAPS
                    unit_at[units[i]] = (tap_done[i], taps_at[i])
            else:
                taps_at = [taps_at[0] + (TAPS + 1) // 2, taps_at[1] + TAPS // 2]
                n_joined += 1
                unit_at[units[0]] = (conv_joined, n_joined)
        for n, unit in enumerate(POOL_UNITS):
            unit_at[unit] = (pool_tap, (TAPS - 1) * (n + 1))
        LOOP_TAPS, LOOP_JOINED = tuple(taps_at), n_joined
        for n in range(NI):
            unit_at[(LOOP_FIRST + n, 1)] = (conv_joined, n_joined + n + 1)
        assert len(unit_at) == KT * NH
        conv_order = [(0, 1, 2, 3, 4, 6, 7, 5), (7, 0, 1, 2, 4, 5, 6, 3)]
        A_UNIT = TAPS - 1

        def tap_cut(n):
            return min(max(5 * (n - 2), 0), 2 * TAPS - 2)

        def out_slot(h, i):
            return (i + 1 - h) % 2

        block = ctx.enter_context(nc.Block())

        @block.sync
        def _(sp):
            def load_pair(par, w, c, gap):
                for g in range(2):
                    sp.dma_start(raw_pair(par)[:, :, g, :], w[:, :, bass.ds(c + g * gap, P)]).then_inc(
                        raw_loaded[par % 2], 16)

            def load_in(par, c):
                sp.dma_start(raw_pair(par)[:, :, 0, :], w_in_v[:, :, bass.ds(c * P + D, P)]).then_inc(raw_loaded[par % 2], 16)
                sp.dma_start(raw_pair(par)[:, :, 1, :], w_in_v[:, :, bass.ds(c * P, P)]).then_inc(raw_loaded[par % 2], 16)

            def load_down(par, r):
                for k in range(2):
                    sp.dma_start(raw[:, par % 2, k * D:(k + 1) * D], w_down_v[:, bass.ds(r + k, 1), :].rearrange(
                        "p k d -> p (k d)")).then_inc(raw_loaded[par % 2], 16)

            def load_out(n, i):
                d, k = i // 2, i % 2
                for j in range(2):
                    k0 = k * KT // 2 + j * 2
                    sp.dma_start(raw[:, n % 2, :].rearrange("p (k c) -> p k c", k=KT // 2)[:, 2 * j:2 * j + 2, :],
                                 w_out_v[:, k0:k0 + 2, d * 512:(d + 1) * 512]).then_inc(raw_loaded[n % 2], 16)

            def raw_free(n):
                sp.wait_ge(raw_lo, n - 1)

            for t in range(TH):
                sp.dma_start(x_in[:, t, :], x_v[t]).then_inc(x_loaded[t], 16)
            load_in(0, 0)
            for t in range(TH, NT):
                sp.dma_start(x_in[:, t, :], x_v[t]).then_inc(x_loaded[t], 16)
            load_in(1, 1)
            with sp.Fori(0, (KT - 2) // 2) as i:
                for j in range(2):
                    raw_free(i * 2 + (2 + j))
                    load_in(j, i * 2 + (2 + j))
            with sp.Fori(0, (KT - 2) // 2) as i:
                for j in range(2):
                    raw_free(i * 2 + (KT + j))
                    load_in(j, i * 2 + j)
            raw_free(2 * KT - 2)
            load_in(2 * KT - 2, KT - 2)
            raw_free(I_BOUT)
            for c in range(2):
                sp.dma_start(raw[0:1, I_BOUT % 2, c * 512:(c + 1) * 512],
                             b_out[:, c * 512:(c + 1) * 512]).then_inc(raw_loaded[I_BOUT % 2], 16)
            for i, n in enumerate(I_OUT[0]):
                raw_free(n)
                load_out(n, i)
                if i == 2:
                    sp.wait_ge(z_lo, KT)
                    sp.dma_start(x2[0], x_v[0:TH].rearrange("t p d -> p t d")).then_inc(x_again[0], 16)

            raw_free(I_IN_LAST)
            load_in(I_IN_LAST, KT - 1)

            def ffn_loads(h):
                F = I_FFN[h]
                for p in range(2):
                    raw_free(F + p)
                    load_pair(F + p, w_up_v, p * P, FF)
                if h == 1:
                    sp.wait_ge(added, NQ * TH)
                    for t in range(TH):
                        sp.dma_start(out_v[t], x2[0][:, t, :]).then_inc(stored, 16)
                with sp.Fori(0, (NQ - 1) // 2) as i:
                    for s in range(2):
                        n = F + 2 + 3 * s
                        for k in range(2):
                            raw_free(i * 6 + (n + k))
                            load_pair(n + k, w_up_v, i * (4 * P) + (2 * s + 2 + k) * P, FF)
                        raw_free(i * 6 + (n + 2))
                        load_down(n + 2, i * 4 + 2 * s)

            ffn_loads(0)
            for i in range(2):
                raw_free(I_OUT[1][i])
                load_out(I_OUT[1][i], i)
            raw_free(I_DOWN_LAST)
            load_down(I_DOWN_LAST, 2 * (NQ - 1))
            sp.wait_ge(z_lo, 2 * KT)
            sp.dma_start(x2[1], x_v[TH:NT].rearrange("t p d -> p t d")).then_inc(x_again[1], 16)
            for i in range(2, 4):
                raw_free(I_OUT[1][i])
                load_out(I_OUT[1][i], i)
            ffn_loads(1)
            raw_free(I_END)
            load_down(I_END, 2 * (NQ - 1))
            for t in range(TH):
                sp.wait_ge(added, (2 * NQ - 1) * TH + t + 1)
                sp.dma_start(out_v[TH + t], x2[1][:, t, :]).then_inc(stored, 16)
            sp.wait_ge(stored, 16 * NT)

        @block.gpsimd
        def _(pool):
            nc.gpsimd.memset(ident[:, :], 0.0).then_inc(ident_zero, 1)
            nc.gpsimd.memset(ones[:, :], 1.0 / D).then_inc(ones_ready, 1)
            nc.gpsimd.memset(one_row[:, :].bitcast(F32), 1.0).then_inc(ones_ready, 1)
            nc.gpsimd.memset(eps, EPS).then_inc(ones_ready, 1)
            pool.wait_ge(ident_zero, 1)
            nc.gpsimd.affine_select(out=ident[:, :], in_=ident[:, :], compare_op=ALU.not_equal, fill=1.0,
                                    base=0, pattern=[[-1, P]], channel_multiplier=1).then_inc(ident_ready, 1)
            nc.gpsimd.memset(u[0][:, :, 0:PAD], 0.0).then_inc(pad_ready, 1)

            def split_lo(n, lo, src, hi):
                pool.wait_ge(raw_hi, n + 1)
                nc.gpsimd.tensor_tensor(lo, src, hi.bitcast(F32), ALU.subtract).then_inc(raw_lo, 1)

            def split_slot(n, par, slot):
                split_lo(n, wsp[:, slot, LO, :], raw[:, par % 2, :], wsp[:, slot, HI, :])

            def split_down(n, par):
                split_lo(n, wd[:, LO, :], raw[:, par % 2, :], wd[:, HI, :])

            def tap(unit, j, turn=0):
                c, h = POOL_UNITS[unit]
                pool.wait_ge(prod_ready, turn * TAPS_A_TURN + (unit * TAPS + j + 1))
                if unit or j > 1:
                    pool.wait_ge(pool_tap, turn * TAPS_A_TURN + (unit * A_UNIT + j - 1))
                before = ring[:, 0, :] if j == 1 else acc_sum[:, :]
                dst = u[h][:, c, PAD:] if j == TAPS - 1 else acc_sum[:, :]
                nc.gpsimd.tensor_tensor(dst, before, ring[:, j % RING, :], ALU.add).then_inc(pool_tap, 1)

            def taps(unit, first, last):
                for j in range(max(first, 1), last):
                    tap(unit, j)

            for n in range(2 * KT - 1):
                split_slot(n, n, n % 2)
                for i in range(tap_cut(n - 1), tap_cut(n)):
                    if i % TAPS:
                        tap(i // TAPS, i % TAPS)
            taps(1, tap_cut(2 * KT - 2) - TAPS, TAPS)
            split_lo(I_BOUT, b_row[:, LO, :], raw[0:1, I_BOUT % 2, 0:D], b_row[:, HI, :])
            split_slot(I_OUT[0][0], I_OUT[0][0], out_slot(0, 0))
            split_slot(I_OUT[0][1], I_OUT[0][1], out_slot(0, 1))
            taps(2, 0, 6)
            split_slot(I_OUT[0][2], I_OUT[0][2], out_slot(0, 2))
            taps(2, 6, 11)
            split_slot(I_OUT[0][3], I_OUT[0][3], out_slot(0, 3))
            taps(2, 11, 16)
            split_slot(I_IN_LAST, I_IN_LAST, 1)
            taps(2, 16, 22)
            split_slot(F0, F0, 0)
            taps(2, 22, TAPS)
            taps(3, 0, TAPS_BEFORE)

            def ffn_splits(h):
                F = I_FFN[h]
                split_slot(F + 1, F + 1, 1)
                turns = NI if h == 0 else (NQ - 1) // 2
                with pool.Fori(0, turns) as i:
                    for s in range(2):
                        n = F + 2 + 3 * s
                        split_slot(i * 6 + n, n, 0)
                        split_slot(i * 6 + (n + 1), n + 1, 1)
                        split_down(i * 6 + (n + 2), n + 2)
                        if h == 0:
                            for j in range(TAPS_A_TURN // 2):
                                tap(3, TAPS_BEFORE + s * (TAPS_A_TURN // 2) + j, i)

            ffn_splits(0)
            for j in range(TAPS_BEFORE + NI * TAPS_A_TURN, TAPS):
                tap(3, j)
            for n in range(F0 + 2 + 6 * NI, last0, 3):
                split_slot(n, n, 0)
                split_slot(n + 1, n + 1, 1)
                split_down(n + 2, n + 2)
            for i in range(4):
                if i == 2:
                    split_down(I_DOWN_LAST, I_DOWN_LAST)
                split_slot(I_OUT[1][i], I_OUT[1][i], out_slot(1, i))
            split_slot(F1, F1, 0)
            ffn_splits(1)
            split_slot(I_END, I_END, 0)

        @block.scalar
        def _(a):
            dwr = dw.rearrange("j (t c) -> (j t) c", c=P)
            ffr = ff_dw.rearrange("j (t c) -> (j t) c", c=P)
            ffb = ff_dw_b.rearrange("o (t c) -> (o t) c", c=P)
            n_dma = 0
            R1, R2 = P, TAPS * KT - P
            for dst, src in ((rows[0:R1, 0, :], dwr[0:R1]), (rows[0:R2, 1, :], dwr[R1:R1 + R2]),
                             (rows[0:4 * NP, 2, :], ffr[0:4 * NP]), (rows[0:2 * NP, 3, :], ffr[4 * NP:6 * NP]),
                             (rows[2 * NP:4 * NP, 3, :], ffb)):
                a.dma_start(dst, src).then_inc(rows_loaded, 16)
                n_dma += 1
            r = 0
            for vec in (norm_mix, norm_ffn, b_in, dw_b, ln_g, ln_b):
                k = vec.shape[1] // P
                a.dma_start(rows[r:r + k, 4, :], vec.rearrange("o (t c) -> (o t) c", c=P)).then_inc(rows_loaded, 16)
                r += k
                n_dma += 1
            assert n_dma == 11

            def split_hi(n, dst, src=None):
                item_ready(a, n)
                src = raw[:, n % 2, :] if src is None else src
                nc.scalar.activation(dst, src, ACT.Copy).then_inc(raw_hi, 1)

            def square(n_before, t, src, junk, waits):
                for w, value in waits:
                    a.wait_ge(w, value)
                if n_before:
                    a.wait_ge(squared, n_before)
                nc.scalar.activation(junk, src, ACT.Square, accum_out=ssq[:, t:t + 1]).then_inc(squared, 1)

            def root(h, n):
                a.wait_ge(squared, n)
                nc.scalar.activation(rms[:, h * TH:(h + 1) * TH], ssq[:, h * TH:(h + 1) * TH], ACT.Sqrt,
                                     bias=eps, scale=1.0 / D).then_inc(rms_ready, 1)

            def turned_hi(stage, slot, gain):
                for k in range(KT):
                    n = stage * KT + k
                    a.wait_ge(turned, n + 1)
                    nc.scalar.activation(hT[:, slot, HI, k, :], ps[:, B_T + n % 4, :], ACT.Copy,
                                         scale=col(gain + k)).then_inc(h_hi, 1)

            a.wait_ge(ones_ready, 3)
            a.wait_ge(pad_ready, 1)
            for t in range(TH):
                square(t, t, x_in[:, t, :], sig_flat, [(x_loaded[t], 16)])
            root(0, TH)
            split_hi(0, wsp[:, 0, HI, :])
            a.wait_ge(cols_ready, 1)
            turned_hi(0, 0, C_NMIX)
            for t in range(TH, NT):
                square(t, t, x_in[:, t, :], sig_flat, [(x_loaded[t], 16)])
            root(1, NT)
            split_hi(1, wsp[:, 1, HI, :])
            turned_hi(1, 1, C_NMIX)

            def sigmoids(c):
                for h in range(NH):
                    a.wait_ge(g_done, c * NH + h + 1)
                    if c:
                        a.wait_ge(glu_done, (c - 1) * NH + 1 + h)
                    nc.scalar.activation(sig[:, h, :], ps[:, B_G + h, :], ACT.Sigmoid,
                                         bias=col(C_BIN + KT + c)).then_inc(sig_done, 1)

            product_at = [0]

            def products(count):
                for i in range(product_at[0], product_at[0] + count):
                    n, j = divmod(i, TAPS)
                    c, h = POOL_UNITS[n]
                    if j == 0:
                        a.wait_ge(glu_done, NH * c + h + 1)
                    if j >= RING:
                        a.wait_ge(pool_tap, n * (TAPS - 1) + max(j - RING, 1))
                    elif n:
                        a.wait_ge(pool_tap, n * (TAPS - 1))
                    src, w = u[h][:, c, j:j + HALF], col(C_DW + j * KT + c)
                    if j == 0:
                        ins = nc.scalar.activation(ring[:, 0, :], src, ACT.Identity, scale=w, bias=col(C_DWB + c))
                    else:
                        ins = nc.scalar.activation(ring[:, j % RING, :], src, ACT.Copy, scale=w)
                    ins.then_inc(prod_ready, 1)
                product_at[0] += count

            def sigmoid(n):
                a.wait_ge(g_done, n + 1)
                if n >= 2:
                    a.wait_ge(glu_done, n - 1)
                nc.scalar.activation(sig[:, n % 2, :], ps[:, B_G + n % 2, :], ACT.Sigmoid,
                                     bias=col(C_BIN + KT + n % KT)).then_inc(sig_done, 1)

            def product(unit, j, turn=0):
                c, h = POOL_UNITS[unit]
                if j == 0:
                    a.wait_ge(glu_done, h * KT + c + 1)
                if j >= RING:
                    a.wait_ge(pool_tap, turn * TAPS_A_TURN + (unit * A_UNIT + max(j - RING, 1)))
                elif unit:
                    a.wait_ge(pool_tap, unit * A_UNIT)
                if j == 0:
                    ins = nc.scalar.activation(ring[:, 0, :], u[h][:, c, 0:HALF], ACT.Identity,
                                               scale=col(C_DW + c), bias=col(C_DWB + c))
                else:
                    src = u_all[:, bass.ds(turn * TAPS_A_TURN + ((h * KT + c) * W + j), HALF)]
                    w = cols[:, bass.ds(turn * (TAPS_A_TURN * KT) + (C_DW + j * KT + c), 1)]
                    ins = nc.scalar.activation(ring[:, j % RING, :], src, ACT.Copy, scale=w)
                ins.then_inc(prod_ready, 1)

            product_at = [0]

            def products(count):
                for i in range(product_at[0], product_at[0] + count):
                    product(i // TAPS, i % TAPS)
                product_at[0] += count

            a.wait_ge(squared, NT)
            for n in range(2 * KT - 2):
                if n:
                    a.wait_ge(a_done, n)
                    split_hi(n + 1, wsp[:, (n + 1) % 2, HI, :])
                sigmoid(n)
                if tap_cut(n + 1):
                    products(tap_cut(n + 1) + 1 - product_at[0])
            products(2 * TAPS - product_at[0])
            split_hi(I_BOUT, b_row[:, HI, :], raw[0:1, I_BOUT % 2, 0:D])
            a.wait_ge(a_done, 2 * KT - 2)
            split_hi(I_OUT[0][0], wsp[:, out_slot(0, 0), HI, :])

            def layernorm_stats(h):
                for k in range(KT):
                    n = h * KT + k
                    a.wait_ge(centred, n + 1)
                    if k >= 2:
                        a.wait_ge(var_added, n - 1)
                    nc.scalar.activation(norm[h][:, k % 2, :], u[h][:, conv_order[h][k], PAD:], ACT.Square).then_inc(sq_done, 1)
                a.wait_ge(var_added, (h + 1) * KT)
                nc.scalar.activation(norm[h][:, 2, :], ps[:, B_VAR[h], :], ACT.Sqrt, bias=eps).then_inc(std_done, 1)

            def silus(h, k0, k1):
                def silu(k, dst, signal):
                    nc.scalar.activation(dst, u[h][:, k, PAD:], ACT.Silu, scale=col(C_LNG + k),
                                         bias=col(C_LNB + k)).then_inc(signal, 1)

                for k in range(k0, k1 + 1):
                    if k < k1:
                        a.wait_ge(scaled, h * KT + k + 1)
                        silu(k, hT[:, 0, HI, k, :], z_hi)
                    if k > k0:
                        a.wait_ge(z_hi, h * KT + k)
                        silu(k - 1, u[h][:, k - 1, PAD:], z_full)

            layernorm_stats(0)
            sigmoid(2 * KT - 2)
            silus(0, 0, KT // 2)
            a.wait_ge(a_done, 2 * KT - 1)
            split_hi(I_OUT[0][1], wsp[:, out_slot(0, 1), HI, :])
            silus(0, KT // 2, KT)
            products(7)
            a.wait_ge(out_read, 1)
            split_hi(I_OUT[0][2], wsp[:, out_slot(0, 2), HI, :])
            products(5)
            a.wait_ge(out_done, TH)
            split_hi(I_OUT[0][3], wsp[:, out_slot(0, 3), HI, :])
            products(5)
            a.wait_ge(out_read, 2)
            split_hi(I_IN_LAST, wsp[:, 1, HI, :])

            def ffn_input(h):
                for t in range(TH):
                    square(NT + h * TH + t, h * TH + t, x2[h][:, t, :], junk[h], [(x2_done, (h * DH + 1) * TH + t + 1)])
                root(h, NT + (h + 1) * TH)
                if h == 0:
                    split_hi(I_FFN[h], wsp[:, 0, HI, :])
                    sigmoid(2 * KT - 1)
                    products(5)
                    a.wait_ge(a_done, 2 * KT)
                split_hi(I_FFN[h] + 1, wsp[:, 1, HI, :])
                turned_hi(2 + h, 1, C_NFFN)
                if h == 0:
                    products(3 * TAPS + TAPS_BEFORE - product_at[0])

            def pair(h, p, par, slot, down_next=None, other_next=None, own_next=None):
                n = p + h * NP
                for g, bank, done, dst, first, free in ((0, B_UPG, upg_done, y_g, g_first, prod_done),
                                                        (1, B_UPV, upv_done, y_v, v_first, act_lo)):
                    a.wait_ge(done, n + 1)
                    f = p + g * NP
                    if h == 0:
                        nc.scalar.activation(tails[:, bass.ds(f * 2, 2)], ps[:, bank, HALF - 2:], ACT.Copy)
                    if not (isinstance(n, int) and n == 0):
                        a.wait_ge(free, n)
                    nc.scalar.activation(dst[:, :], ps[:, bank, :], ACT.Identity,
                                         scale=cols[:, bass.ds(f + (C_FF + 2 * 2 * NP), 1)],
                                         bias=cols[:, bass.ds(f + (C_FF + 3 * 2 * NP), 1)]).then_inc(first, 1)
                    if g == 0:
                        split_item(down_next, wd[:, HI, :])
                        split_item(other_next, wsp[:, 1 - par, HI, :])
                a.wait_ge(g_taps, n + 1)
                nc.scalar.activation(y_g[:, :], y_g[:, :], ACT.Silu).then_inc(silu_done, 1)
                a.wait_ge(prod_done, n + 1)
                nc.scalar.activation(act[:, slot, par, HI, :], y_v[:, :], ACT.Copy).then_inc(act_hi, 1)
                split_item(own_next, wsp[:, par, HI, :])

            def split_item(what, dst):
                if what is not None:
                    count, n = what
                    a.wait_ge(raw_loaded[n % 2], count)
                    nc.scalar.activation(dst, raw[:, n % 2, :], ACT.Copy).then_inc(raw_hi, 1)

            def item(n, i=0):
                return i * 96 + (n // 2 + 1) * 32, n

            def group(h, q, s, i=0, work=(), last=False):
                n = I_FFN[h] + 2 + 3 * s
                pair(h, q * 2, 0, (s + 1) % 2, down_next=item(n + 2, i))
                if work:
                    work[0]()
                pair(h, q * 2 + 1, 1, (s + 1) % 2, other_next=item(n + 3, i),
                     own_next=None if last else item(n + 4, i))
                if work:
                    work[1]()

            def first_pairs(h):
                pair(h, 0, 0, 0)
                pair(h, 1, 1, 0, other_next=item(I_FFN[h] + 2), own_next=item(I_FFN[h] + 3))

            ffn_input(0)
            first_pairs(0)
            def tap_products(s, i):
                for j in range(TAPS_A_TURN // 2):
                    product(3, TAPS_BEFORE + s * (TAPS_A_TURN // 2) + j, i)

            with a.Fori(0, NI) as i:
                for s in range(2):
                    group(0, i * 2 + (s + 1), s, i, (lambda: tap_products(s, i), lambda: None))
            for j in range(TAPS_BEFORE + NI * TAPS_A_TURN, TAPS):
                product(3, j)
            layernorm_stats(1)
            group(0, NQ - 2, 2 * NI, 0, (lambda: silus(1, 0, 4), lambda: silus(1, 4, KT)))
            group(0, NQ - 1, 2 * NI + 1)
            a.wait_ge(down_done, (NQ - 1) * TH)
            split_hi(I_DOWN_LAST, wd[:, HI, :])
            a.wait_ge(out_read, 3)
            split_hi(I_OUT[1][2], wsp[:, out_slot(1, 2), HI, :])
            a.wait_ge(out_done, 3 * TH)
            split_hi(I_OUT[1][3], wsp[:, out_slot(1, 3), HI, :])
            a.wait_ge(out_read, 4)
            split_hi(F1, wsp[:, 0, HI, :])
            ffn_input(1)
            first_pairs(1)
            with a.Fori(0, (NQ - 3) // 2) as i:
                for s in range(2):
                    group(1, i * 2 + (s + 1), s, i)
            group(1, NQ - 2, NQ - 3)
            group(1, NQ - 1, NQ - 2, last=True)

        @block.vector
        def _(dve):
            v = nc.vector

            def diagonals(stage, h, waits):
                dve.wait_ge(rms_ready, stage + 1)
                v.reciprocal(rrms[:, h * TH:(h + 1) * TH], rms[:, h * TH:(h + 1) * TH]).then_inc(rrms_ready, 1)
                for w, value in waits:
                    dve.wait_ge(w, value)
                dve.wait_ge(rrms_ready, stage + 1)
                for t in range(TH):
                    ins = v.tensor_scalar(diag[:, t * P:(t + 1) * P], ident[:, :],
                                          rrms[:, h * TH + t:h * TH + t + 1], None, ALU.mult)
                ins.then_inc(diag_ready, 1)

            def turned_lo(stage, slot, gain):
                for k in range(KT):
                    n = stage * KT + k
                    dve.wait_ge(h_hi, n + 1)
                    v.scalar_tensor_tensor(out=hT[:, slot, LO, k, :], in0=ps[:, B_T + n % 4, :], scalar=col(gain + k),
                                           in1=hT[:, slot, HI, k, :].bitcast(F32), op0=ALU.mult,
                                           op1=ALU.subtract).then_inc(h_lo, 1)

            def glu(n):
                h, c = divmod(n, KT)
                dve.wait_ge(sig_done, n + 1)
                dve.wait_ge(a_done, n + 1)
                spots = [(u[h][:, c, PAD:], 0)]
                if h == 0:
                    spots.insert(0, (u[1][:, c, 0:PAD], HALF - PAD))
                for dst, s in spots:
                    ins = v.scalar_tensor_tensor(out=dst, in0=ps[:, B_A + n % 2, s:], scalar=col(C_BIN + c),
                                                 in1=sig[:, n % 2, s:], op0=ALU.add, op1=ALU.mult)
                ins.then_inc(glu_done, 1)

            taps_done = [0, 0]
            joined = [0]

            def conv(n, hooks=None):
                units = CHAINS[n]
                if len(units) == 2:
                    chains = [(unit, range(TAPS)) for unit in units]
                else:
                    chains = [(units[0], range(0, TAPS, 2)), (units[0], range(1, TAPS, 2))]
                for step in range(len(chains[0][1])):
                    for i, ((c, h), taps) in enumerate(chains):
                        if step >= len(taps):
                            continue
                        j = taps[step]
                        if taps_done[i]:
                            dve.wait_ge(tap_done[i], taps_done[i])
                        if step == 0:
                            dve.wait_ge(glu_done, h * KT + c + 1)
                        if step == 0 and joined[0]:
                            dve.wait_ge(conv_joined, joined[0])
                        acc = ps[:, B_CONV + i, :]
                        src, w = u[h][:, c, j:j + HALF], col(C_DW + j * KT + c)
                        if j == 0:
                            ins = v.tensor_scalar(acc, src, w, col(C_DWB + c), ALU.mult, ALU.add)
                        elif step == 0:
                            ins = v.tensor_scalar(acc, src, w, None, ALU.mult)
                        else:
                            dst = src if j == TAPS - 1 else acc
                            if j == TAPS - 1 and len(units) == 1:
                                dve.wait_ge(tap_done[1], taps_done[1])
                            ins = v.scalar_tensor_tensor(out=dst, in0=src, scalar=w, in1=acc,
                                                         op0=ALU.mult, op1=ALU.add)
                        ins.then_inc(tap_done[i], 1)
                        taps_done[i] += 1
                    for work in (hooks or {}).get(step, ()):
                        work()
                if len(units) == 1:
                    c, h = units[0]
                    dve.wait_ge(tap_done[0], taps_done[0])
                    v.tensor_tensor(u[h][:, c, PAD:], u[h][:, c, PAD:], ps[:, B_CONV + 1, :],
                                    ALU.add).then_inc(conv_joined, 1)
                    joined[0] += 1

            def centre(h):
                dve.wait_ge(mean_done, h + 1)
                for c in conv_order[h]:
                    v.tensor_tensor(u[h][:, c, PAD:], u[h][:, c, PAD:], ps[:, B_MEAN[h], :],
                                    ALU.subtract).then_inc(centred, 1)

            def scale(h):
                dve.wait_ge(std_done, h + 1)
                v.reciprocal(norm[h][:, 3, :], norm[h][:, 2, :]).then_inc(rstd_done, 1)
                dve.wait_ge(rstd_done, h + 1)
                for k in range(KT):
                    v.tensor_tensor(u[h][:, k, PAD:], u[h][:, k, PAD:], norm[h][:, 3, :], ALU.mult).then_inc(scaled, 1)

            def z_low(h, k0, k1):
                for k in range(k0, k1):
                    dve.wait_ge(z_full, h * KT + k + 1)
                    v.tensor_tensor(hT[:, 0, LO, k, :], u[h][:, k, PAD:], hT[:, 0, HI, k, :].bitcast(F32),
                                    ALU.subtract).then_inc(z_lo, 1)

            def add_out(h, i):
                d, t = divmod(i, TH)
                dve.wait_ge(out_done, h * DH * TH + i + 1)
                dve.wait_ge(x_again[h], 16)
                x2_t = x2[h][:, t, d * 512:(d + 1) * 512]
                v.tensor_tensor(x2_t, x2_t, ps[:, t, :], ALU.add).then_inc(x2_done, 1)

            dve.wait_ge(cols_turned, 1)
            v.tensor_copy(cols[:, :], ps[:, 0, 0:NCOLS]).then_inc(cols_ready, 1)
            dve.wait_ge(ident_ready, 1)
            diagonals(0, 0, [(cols_ready, 1)])
            turned_lo(0, 0, C_NMIX)
            diagonals(1, 1, [(turned, KT)])
            turned_lo(1, 1, C_NMIX)
            glu(0)
            dve.wait_ge(pad_ready, 1)

            def at(first, every, works):
                return {first + every * i: [w] for i, w in enumerate(works)}

            def glus(a, b):
                return [lambda n=n: glu(n) for n in range(a, b)]

            conv(0, at(7, 8, glus(1, 3)))
            conv(1, at(6, 8, glus(3, 5)))
            conv(2, at(6, 8, glus(5, 9)))
            conv(3, at(5, 8, glus(9, 13)))
            glu(2 * KT - 3)
            centre(0)
            scale(0)
            glu(2 * KT - 2)
            z_low(0, 0, KT)
            adds = [lambda n=n: add_out(0, n) for n in range(DH * TH)]
            conv(4, {**at(8, 2, adds[:TH]), **at(23, 2, adds[TH:])})

            def ffn_input(h):
                diagonals(2 + h, h, [(turned, (2 + h) * KT)])
                if h == 0:
                    glu(2 * KT - 1)
                turned_lo(2 + h, 1, C_NFFN)

            def later_taps(h, p, g, bank, y, first, second, done):
                n = p + h * NP
                f = p + g * NP
                w1 = cols[:, bass.ds(f + (C_FF + 2 * NP), 1)]
                w0 = cols[:, bass.ds(f + C_FF, 1)]
                dve.wait_ge(first, n + 1)

                def tap(dst, src, w):
                    return v.scalar_tensor_tensor(out=dst, in0=src, scalar=w, in1=dst, op0=ALU.mult, op1=ALU.add)

                if h:
                    tap(y[:, 0:1], tails[:, bass.ds(f * 2 + 1, 1)], w1)
                tap(y[:, 1:], ps[:, bank, 0:HALF - 1], w1).then_inc(second, 1)
                dve.wait_ge(second, n + 1)
                if h:
                    tap(y[:, 0:2], tails[:, bass.ds(f * 2, 2)], w0)
                tap(y[:, 2:], ps[:, bank, 0:HALF - 2], w0).then_inc(done, 1)

            def add_down(h, n, t):
                dve.wait_ge(down_done, n + 1)
                v.tensor_tensor(x2[h][:, t, :], x2[h][:, t, :], banks(B_DOWN + 2 * (t % 2)), ALU.add).then_inc(added, 1)

            def pair(h, p, par, slot, down_of=None, conv_taps=lambda n: None):
                n = p + h * NP
                adds = [] if down_of is None else list(range(TH))

                def add():
                    if adds:
                        t = adds.pop(0)
                        add_down(h, down_of * TH + t, t)

                later_taps(h, p, 0, B_UPG, y_g, g_first, g_second, g_taps)
                conv_taps(4)
                later_taps(h, p, 1, B_UPV, y_v, v_first, v_second, v_taps)
                dve.wait_ge(silu_done, n + 1)
                dve.wait_ge(v_taps, n + 1)
                v.tensor_tensor(y_v[:, :], y_g[:, :], y_v[:, :], ALU.mult).then_inc(prod_done, 1)
                add()
                dve.wait_ge(act_hi, n + 1)
                v.tensor_tensor(act[:, slot, par, LO, :], y_v[:, :], act[:, slot, par, HI, :].bitcast(F32),
                                ALU.subtract).then_inc(act_lo, 1)
                while adds:
                    add()
                conv_taps(4)

            def group(h, q, s, conv_taps=lambda n: None, between=lambda: None):
                pair(h, q * 2, 0, (s + 1) % 2, conv_taps=conv_taps)
                between()
                pair(h, q * 2 + 1, 1, (s + 1) % 2, down_of=q + (h * NQ - 1), conv_taps=conv_taps)

            ffn_input(0)
            pair(0, 0, 0, 0)
            pair(0, 1, 1, 0)
            with dve.Fori(0, NI) as i:
                next_tap = [0]

                def conv_taps(count):
                    for j in range(next_tap[0], min(next_tap[0] + count, TAPS)):
                        e = j % 2
                        per_turn = (TAPS + 1 - e) // 2
                        dve.wait_ge(tap_done[e], i * per_turn + (LOOP_TAPS[e] + j // 2))
                        if j < 2:
                            dve.wait_ge(conv_joined, i + LOOP_JOINED)
                        acc = ps[:, B_LOOP + e, :]
                        src = u_all[:, bass.ds(i * W + ((KT + LOOP_FIRST) * W + j), HALF)]
                        w = cols[:, bass.ds(i + (C_DW + j * KT + LOOP_FIRST), 1)]
                        if j == 0:
                            ins = v.tensor_scalar(acc, src, w, cols[:, bass.ds(i + (C_DWB + LOOP_FIRST), 1)],
                                                  ALU.mult, ALU.add)
                        elif j == 1:
                            ins = v.tensor_scalar(acc, src, w, None, ALU.mult)
                        else:
                            if j == TAPS - 1:
                                dve.wait_ge(tap_done[1], i * (TAPS // 2) + (LOOP_TAPS[1] + TAPS // 2))
                            ins = v.scalar_tensor_tensor(out=src if j == TAPS - 1 else acc, in0=src, scalar=w,
                                                         in1=acc, op0=ALU.mult, op1=ALU.add)
                        ins.then_inc(tap_done[e], 1)
                        if j == TAPS - 1:
                            dve.wait_ge(tap_done[0], i * per_turn + (LOOP_TAPS[0] + per_turn))
                            v.tensor_tensor(src, src, ps[:, B_LOOP + 1, :], ALU.add).then_inc(conv_joined, 1)
                    next_tap[0] += count

                for s in range(2):
                    group(0, i * 2 + (s + 1), s, conv_taps)
            centre(1)
            group(0, NQ - 2, 2 * NI, between=lambda: scale(1))
            z_low(1, 0, 4)
            group(0, NQ - 1, 2 * NI + 1, between=lambda: z_low(1, 4, KT))
            for n in range(DH * TH):
                add_out(1, n)
            for t in range(TH):
                add_down(0, (NQ - 1) * TH + t, t)
            ffn_input(1)
            pair(1, 0, 0, 0)
            pair(1, 1, 1, 0)
            with dve.Fori(0, (NQ - 1) // 2) as i:
                for s in range(2):
                    group(1, i * 2 + (s + 1), s)
            for t in range(TH):
                add_down(1, (2 * NQ - 1) * TH + t, t)

        @block.tensor
        def _(pe):
            mm = nc.tensor.matmul
            PASSES = ((HI, HI), (HI, LO), (LO, HI))

            def turn(stage, src):
                pe.wait_ge(diag_ready, stage + 1)
                for k in range(KT):
                    n = stage * KT + k
                    if n >= 4:
                        pe.wait_ge(h_lo, n - 3)
                    for t in range(TH):
                        ins = mm(ps[:, B_T + n % 4, t * P:(t + 1) * P], src[:, t, k * P:(k + 1) * P],
                                 diag[:, t * P:(t + 1) * P], start=True, stop=True)
                    ins.then_inc(turned, 1)

            def project(bank, slot, g, x_slot, signal, each=None):
                for k in range(KT):
                    if each is not None:
                        pe.wait_ge(h_lo, each + k + 1)
                    for n, (pw, px) in enumerate(PASSES):
                        ins = mm(ps[:, bank, :], wtile(slot, pw, k, g), hT[:, x_slot, px, k, :],
                                 start=(k == 0 and n == 0), stop=(k == KT - 1 and n == 2))
                ins.then_inc(signal, 1)

            def in_pair(n, par, h, item_=None, after=None):
                pe.wait_ge(raw_lo, (n if item_ is None else item_) + 1)
                for i, (bank, g, free, signal) in enumerate(((B_G, 0, sig_done, g_done), (B_A, 1, glu_done, a_done))):
                    if after is None:
                        pe.wait_ge(free, n - 1)
                    else:
                        pe.wait_ge(*after[i])
                    project(bank + par, par, g, h, signal)

            pe.wait_ge(ident_ready, 1)
            pe.wait_ge(rows_loaded, 11 * 16)
            at = 0
            for r, k in enumerate((P, TAPS * KT - P, 4 * NP, 4 * NP, 7 * KT)):
                ins = nc.tensor.transpose(ps[:, 0, at:at + k], rows[0:k, r, :], ident[0:k, 0:k])
                at += k
            assert at == NCOLS
            ins.then_inc(cols_turned, 1)

            pe.wait_ge(ones_ready, 3)
            for n in range(2):
                turn(n, x_in[:, n * TH:(n + 1) * TH, :])
                pe.wait_ge(cols_ready, 1)
                pe.wait_ge(raw_lo, n + 1)
                project(B_G + n, n, 0, 0, g_done, each=n * KT)
                project(B_A + n, n, 1, 0, a_done)
            with pe.Fori(2, KT, 2) as n:
                in_pair(n, 0, 0)
                in_pair(n + 1, 1, 0)
            with pe.Fori(KT, 2 * KT - 2, 2) as n:
                in_pair(n, 0, 1)
                in_pair(n + 1, 1, 1)

            def statistics(h):
                for n, c in enumerate(conv_order[h]):
                    s, value = unit_at[(c, h)]
                    pe.wait_ge(s, value)
                    ins = mm(ps[:, B_MEAN[h], :], ones[:, :], u[h][:, c, PAD:], start=(n == 0), stop=(n == KT - 1))
                ins.then_inc(mean_done, 1)
                for k in range(KT):
                    n = h * KT + k
                    pe.wait_ge(sq_done, n + 1)
                    mm(ps[:, B_VAR[h], :], ones[:, :], norm[h][:, k % 2, :], start=(k == 0),
                       stop=(k == KT - 1)).then_inc(var_added, 1)

            def project_out(h):
                for i, n in enumerate(I_OUT[h]):
                    d, kh = divmod(i, 2)
                    pe.wait_ge(raw_lo, n + 1)
                    for t in range(TH):
                        if d and not kh:
                            pe.wait_ge(x2_done, h * DH * TH + t + 1)
                        elif h == 0 and not kh:
                            pe.wait_ge((sig_done, glu_done)[t // 2], 2 * KT - 1 - t % 2)
                        if t == 0 and d == 0:
                            pe.wait_ge(z_lo, h * KT + (kh + 1) * KT // 2)
                        for k in range(KT // 2):
                            for m, (pz, pw) in enumerate(PASSES):
                                ins = mm(ps[:, t, :], hT[:, 0, pz, kh * KT // 2 + k, t * P:(t + 1) * P],
                                         wsp[:, out_slot(h, i), pw, k * 512:(k + 1) * 512],
                                         start=(not kh and k == 0 and m == 0), stop=False)
                        if t == TH - 1 and not kh:
                            ins.then_inc(out_read, 1)
                        if kh:
                            for part in (HI, LO):
                                ins = mm(ps[:, t, :], one_row[:, :], b_row[:, part, d * 512:(d + 1) * 512],
                                         start=False, stop=(part == LO))
                            ins.then_inc(out_done, 1)

            statistics(0)
            in_pair(2 * KT - 2, 0, 1)
            project_out(0)
            in_pair(2 * KT - 1, 1, 1, I_IN_LAST, ((x2_done, DH * TH - 2), (x2_done, DH * TH)))

            def down(n, slot, weights, t_free=2):
                pe.wait_ge(act_lo, n * 2 + 2)
                for t in range(TH):
                    if t >= t_free:
                        pe.wait_ge(added, n * TH + (t - 1))
                    for b in range(DH):
                        for k in range(2):
                            for m, (pa, pw) in enumerate(PASSES):
                                o = k * D + b * 512
                                ins = mm(ps[:, B_DOWN + 2 * (t % 2) + b, :], act[:, slot, k, pa, t * P:(t + 1) * P],
                                         weights(pw, o), start=(k == 0 and m == 0), stop=(k == 1 and m == 2))
                    ins.then_inc(down_done, 1)

            def in_wd(part, o):
                return wd[:, part, o:o + 512]

            def up_pair(n, item_, slot):
                pe.wait_ge(raw_lo, item_ + 1)
                for bank, g, free, signal in ((B_UPG, 0, g_taps, upg_done), (B_UPV, 1, v_taps, upv_done)):
                    pe.wait_ge(free, n)
                    project(bank, slot, g, 1, signal)

            def group(h, q, item_, s):
                up_pair(q * 2 + h * NP, item_, 0)
                up_pair(q * 2 + (h * NP + 1), item_ + 1, 1)
                pe.wait_ge(raw_lo, item_ + 3)
                down(q + (h * NQ - 1), s % 2, in_wd)

            def first_pairs(h):
                turn(2 + h, x2[h])
                pe.wait_ge(x2_done, (h + 1) * DH * TH)
                pe.wait_ge(raw_lo, I_FFN[h] + 1)
                project(B_UPG, 0, 0, 1, upg_done, each=(2 + h) * KT)
                project(B_UPV, 0, 1, 1, upv_done)
                up_pair(h * NP + 1, I_FFN[h] + 1, 1)

            first_pairs(0)
            with pe.Fori(0, NI) as i:
                for s in range(2):
                    group(0, i * 2 + (s + 1), i * 6 + (F0 + 2 + 3 * s), s)
            statistics(1)
            for q in (NQ - 2, NQ - 1):
                group(0, q, F0 + 2 + 3 * (q - 1), q - 1)
            project_out(1)
            pe.wait_ge(raw_lo, I_DOWN_LAST + 1)
            pe.wait_ge(added, (NQ - 1) * TH)
            down(NQ - 1, 0, in_wd)
            pe.wait_ge(added, NQ * TH)
            first_pairs(1)
            with pe.Fori(0, (NQ - 1) // 2) as i:
                for s in range(2):
                    group(1, i * 2 + (s + 1), i * 6 + (F1 + 2 + 3 * s), s)
            pe.wait_ge(raw_lo, I_END + 1)
            pe.wait_ge(added, (2 * NQ - 1) * TH)
            down(2 * NQ - 1, 0, lambda part, o: wsp[:, 0, part, o:o + 512])


_INS = ["x", "norm_mix", "norm_ffn", "cm_w_in", "cm_b_in", "cm_dw", "cm_dw_b", "cm_ln_g", "cm_ln_b",
        "cm_w_out", "cm_b_out", "ff_w_up", "ff_dw", "ff_dw_b", "ff_w_down"]


def kernel(**inputs):
    import numpy as np
    import concourse.bacc as bacc
    from concourse.bass_utils import run_bass_kernel_spmd

    nc = bacc.Bacc("TRN2", target_bir_lowering=False, num_devices=1)
    arrays, args = {}, []
    for name in _INS:
        a = np.ascontiguousarray(inputs[name])
        arrays[f"in_{name}"] = a
        ap = nc.dram_tensor(f"in_{name}", a.shape, mybir.dt.from_np(a.dtype), kind="ExternalInput").ap()
        args.append(ap if len(a.shape) == 2 else ap.rearrange("o a b -> (o a) b"))
    shape = inputs["x"].shape
    out = nc.dram_tensor("out", shape, F32, kind="ExternalOutput").ap()
    conformer_ffn(nc, *args, out.rearrange("o a b -> (o a) b"))
    r = run_bass_kernel_spmd(nc, [arrays], core_ids=[0])
    return r.results[0]["out"]
```

```python
from contextlib import ExitStack

import concourse.bass as bass
from concourse import mybir

F32 = mybir.dt.float32
F32R = mybir.dt.float32r
ALU = mybir.AluOpType
ACT = mybir.ActivationFunctionType

P = 128
EPS = 1e-6
HI, LO = 0, 1


def conformer_ffn(nc, x, norm_mix, norm_ffn, w_in, b_in, dw, dw_b, ln_g, ln_b, w_out, b_out,
                  w_up, ff_dw, ff_dw_b, w_down, out):
    SEQ, D = x.shape
    KT = D // P
    HALF = 512
    NH = SEQ // HALF
    TH = HALF // P
    NT = SEQ // P
    TAPS = dw.shape[0]
    PAD = TAPS - 1
    FFK = ff_dw.shape[0]
    FF = w_down.shape[0]
    NP = FF // P
    NQ = NP // 2
    DH = D // 512
    assert NH == 2 and KT == 8 and DH == 2 and FFK == 3 and NP == 22

    CHAINS = [((0, 0),), ((2, 0),), ((3, 0), (4, 0)), ((6, 0), (7, 0)), ((0, 1), (1, 1))]
    POOL_UNITS = [(1, 0), (5, 0), (2, 1), (3, 1)]
    LOOP_FIRST = 4
    RING = 3
    MIXED, MIXED_FROM = 1, 24
    POOL_TAPS = [MIXED_FROM if n == MIXED else TAPS for n in range(len(POOL_UNITS))]
    TAPS_BEFORE, TAPS_A_TURN = 6, 6
    assert TAPS_BEFORE % RING == 0 and TAPS_A_TURN % RING == 0
    NI = (NQ - 3) // 2

    x_v = x.rearrange("(t p) d -> t p d", p=P)
    out_v = out.rearrange("(t p) d -> t p d", p=P)
    w_in_v = w_in.rearrange("(k p) n -> p k n", p=P)
    w_out_v = w_out.rearrange("(k p) n -> p k n", p=P)
    w_up_v = w_up.rearrange("(k p) n -> p k n", p=P)
    w_down_v = w_down.rearrange("(k p) n -> p k n", p=P)

    ctx = ExitStack()
    with ctx:
        def sb(name, shape, dt=F32):
            return ctx.enter_context(nc.sbuf_tensor(name, shape, dt))

        def sem(name):
            return ctx.enter_context(nc.semaphore(name))

        ITEM = KT * 2 * P
        W = PAD + HALF
        work_at = nc.sbuf_base + -nc.sbuf_base % 32
        work = sb("work", [P, 14336])
        hT = sb("hT", [P, NH, 2, KT, HALF], F32R)
        u_all = sb("u_all", [P, NH * KT * W])
        raw = sb("raw", [P, 2, ITEM])
        wsp = sb("wsp", [P, 2, 2, ITEM], F32R)
        cols = sb("cols", [P, 480])
        ident = sb("ident", [P, P])
        ones = sb("ones", [P, P])
        one_rows = sb("one_rows", [2, P], F32R)
        acc_sum = sb("acc_sum", [P, HALF])
        small = sb("small", [P, 32])
        tails = sb("tails", [P, 2 * NP * (FFK - 1)])

        def over(byte, name, shape, dt=F32):
            size = 4
            for n in shape[1:]:
                size *= n
            assert byte + size <= 14336 * 4
            return nc.alloc_sbuf_tensor_at(name, shape, dt, offset=work_at + byte)

        x_in = over(0, "x_in", [P, NT, D])
        rows = over(36864, "rows", [P, 5, P])
        sig = over(53248, "sig", [P, NH, HALF])
        diag = over(32768, "diag", [P, HALF])
        act = over(0, "act", [P, 2, 2, 2, HALF], F32R)
        wd = over(16384, "wd", [P, 2, ITEM], F32R)
        y_g = over(32768, "y_g", [P, HALF])
        y_v = over(34816, "y_v", [P, HALF])
        ring = over(36864, "ring", [P, RING, HALF])
        N_STD, N_RSTD = 2, 3
        norm = [over(at, f"norm{h}", [P, n, HALF]) for h, (at, n) in enumerate(((0, 4 + KT), (36864, 4)))]
        tile_sum = norm[1][:, N_RSTD, :]
        squares = [[norm[0][:, 4 + k, :] for k in range(KT)],
                   [norm[1][:, 0, :], norm[1][:, 1, :], sig[:, 0, :], sig[:, 1, :]] * 2]
        b_rows = over(45056, "b_rows", [2, D], F32R)
        b_hi = over(49152, "b_hi", [2, D], F32R)

        u = [u_all[:, h * KT * W:(h + 1) * KT * W].rearrange("p (k s) -> p k s", k=KT) for h in range(NH)]
        x2 = [u_all[:, h * KT * W:h * KT * W + TH * D].rearrange("p (t d) -> p t d", t=TH) for h in range(NH)]
        sig_flat = sig[:, :, :].rearrange("p h s -> p (h s)")
        junk = [norm[h][:, 0:2, :].rearrange("p n s -> p (n s)") for h in range(NH)]

        def banks(b):
            return ps[:, b:b + 2, :].rearrange("p b s -> p (b s)")

        def raw_pair(n):
            return raw[:, n % 2, :].rearrange("p (k g c) -> p k g c", k=KT, g=2)

        def wtile(slot, part, k, g):
            o = (k * 2 + g) * P
            return wsp[:, slot, part, o:o + P]

        C_DW, C_FF = 0, TAPS * KT
        C_NMIX = C_FF + (FFK + 1) * 2 * NP
        C_NFFN, C_BIN, C_DWB, C_LNG, C_LNB = (C_NMIX + KT * n for n in (1, 2, 4, 5, 6))
        NCOLS = C_LNB + KT
        assert NCOLS == 480

        def col(n):
            return cols[:, n:n + 1]

        ssq, rms, rrms, eps = small[:, 0:NT], small[:, 8:16], small[:, 16:24], small[:, 24:25]

        ps = ctx.enter_context(nc.psum_tensor("ps", [P, 8, HALF], F32))
        B_G, B_A, B_CONV, B_T, B_DOWN = 0, 2, 4, 4, 4
        B_MEAN, B_VAR, B_MIXED = (6, 3), (7, 2), 7
        B_COLS = (0, 3)
        B_UPG, B_UPV, B_LOOP = 0, 1, 2

        x_loaded = [sem(f"x_loaded{t}") for t in range(NT)]
        vectors_loaded, taps_loaded = sem("vectors_loaded"), sem("taps_loaded")
        raw_loaded = [sem(f"raw_loaded{b}") for b in range(2)]
        x_again = [sem(f"x_again{h}") for h in range(NH)]
        stored = sem("stored")
        ident_zero, ident_ready, ones_ready, pad_ready = (
            sem("ident_zero"), sem("ident_ready"), sem("ones_ready"), sem("pad_ready"))
        cols_turned, cols_ready = sem("cols_turned"), sem("cols_ready")
        raw_hi, raw_lo = sem("raw_hi"), sem("raw_lo")
        squared, rms_ready, rrms_ready, diag_ready = (
            sem("squared"), sem("rms_ready"), sem("rrms_ready"), sem("diag_ready"))
        turned, h_hi, h_lo = sem("turned"), sem("h_hi"), sem("h_lo")
        g_done, a_done, sig_done, glu_done = sem("g_done"), sem("a_done"), sem("sig_done"), sem("glu_done")
        tap_done = [sem("tap_done0"), sem("tap_done1")]
        conv_joined, prod_ready, pool_tap = sem("conv_joined"), sem("prod_ready"), sem("pool_tap")
        mean_done, centred, sq_done, var_added, std_done, rstd_done, scaled = (
            sem("mean_done"), sem("centred"), sem("sq_done"), sem("var_added"), sem("std_done"),
            sem("rstd_done"), sem("scaled"))
        b_ready = sem("b_ready")
        mixed_tap, summed, sq_summed = sem("mixed_tap"), sem("summed"), sem("sq_summed")
        z_hi, z_full, z_lo = sem("z_hi"), sem("z_full"), sem("z_lo")
        out_read, out_done, x2_done = sem("out_read"), sem("out_done"), sem("x2_done")
        upg_done, upv_done, down_done, added = sem("upg_done"), sem("upv_done"), sem("down_done"), sem("added")
        g_first, g_second, g_taps, v_first, v_second, v_taps = (
            sem("g_first"), sem("g_second"), sem("g_taps"), sem("v_first"), sem("v_second"), sem("v_taps"))
        silu_done, prod_done, act_hi, act_lo = (
            sem("silu_done"), sem("prod_done"), sem("act_hi"), sem("act_lo"))

        I_BOUT = 2 * KT - 1
        I_OUT = (tuple(range(I_BOUT + 1, I_BOUT + 5)), )
        I_IN_LAST = I_BOUT + 5
        F0 = I_IN_LAST + 1
        last0 = F0 + 2 + 3 * (NQ - 1)
        I_OUT += ((last0, last0 + 1, last0 + 3, last0 + 4), )
        I_DOWN_LAST = last0 + 2
        F1 = last0 + 5
        I_FFN = (F0, F1)
        I_END = F1 + 2 + 3 * (NQ - 1)

        def item_ready(eng, n):
            eng.wait_ge(raw_loaded[n % 2], (n // 2 + 1) * 32)


        unit_at, taps_at, n_joined = {}, [0, 0], 0
        for units in CHAINS:
            if len(units) == 2:
                for i in range(2):
                    taps_at[i] += TAPS
                    unit_at[units[i]] = (tap_done[i], taps_at[i])
            else:
                taps_at = [taps_at[0] + (TAPS + 1) // 2, taps_at[1] + TAPS // 2]
                n_joined += 1
                unit_at[units[0]] = (conv_joined, n_joined)
        n_joined += 1
        unit_at[POOL_UNITS[MIXED]] = (conv_joined, n_joined)
        PROD0 = [sum(POOL_TAPS[:n]) for n in range(len(POOL_UNITS) + 1)]
        TAP0 = [sum(POOL_TAPS[:n]) - n for n in range(len(POOL_UNITS) + 1)]
        for n, unit in enumerate(POOL_UNITS):
            if n != MIXED:
                unit_at[unit] = (pool_tap, TAP0[n + 1])
        LOOP_TAPS, LOOP_JOINED = tuple(taps_at), n_joined
        for n in range(NI):
            unit_at[(LOOP_FIRST + n, 1)] = (conv_joined, n_joined + n + 1)
        assert len(unit_at) == KT * NH
        conv_order = [(0, 1, 2, 3, 4, 6, 7, 5), tuple(range(KT))]

        def tap_cut(n):
            return 4 * n - 6 if n > 1 else 0

        assert TAPS < tap_cut(2 * KT - 3) < PROD0[2]

        def out_slot(h, i):
            return (i + 1 - h) % 2

        block = ctx.enter_context(nc.Block())

        @block.sync
        def _(sp):
            def load_pair(par, w, c, gap):
                for g in range(2):
                    sp.dma_start(raw_pair(par)[:, :, g, :], w[:, :, bass.ds(c + g * gap, P)]).then_inc(
                        raw_loaded[par % 2], 16)

            def load_in(par, c):
                sp.dma_start(raw_pair(par)[:, :, 0, :], w_in_v[:, :, bass.ds(c * P + D, P)]).then_inc(raw_loaded[par % 2], 16)
                sp.dma_start(raw_pair(par)[:, :, 1, :], w_in_v[:, :, bass.ds(c * P, P)]).then_inc(raw_loaded[par % 2], 16)

            def load_down(par, r):
                for k in range(2):
                    sp.dma_start(raw[:, par % 2, k * D:(k + 1) * D], w_down_v[:, bass.ds(r + k, 1), :].rearrange(
                        "p k d -> p (k d)")).then_inc(raw_loaded[par % 2], 16)

            def load_out(n, i):
                d, k = i // 2, i % 2
                for j in range(2):
                    k0 = k * KT // 2 + j * 2
                    sp.dma_start(raw[:, n % 2, :].rearrange("p (k c) -> p k c", k=KT // 2)[:, 2 * j:2 * j + 2, :],
                                 w_out_v[:, k0:k0 + 2, d * 512:(d + 1) * 512]).then_inc(raw_loaded[n % 2], 16)

            def raw_free(n):
                sp.wait_ge(raw_lo, n - 1)

            for t in range(TH):
                sp.dma_start(x_in[:, t, :], x_v[t]).then_inc(x_loaded[t], 16)
            r = 0
            for vec in (norm_mix, norm_ffn, b_in, dw_b, ln_g, ln_b):
                k = vec.shape[1] // P
                sp.dma_start(rows[r:r + k, 4, :], vec.rearrange("o (t c) -> (o t) c", c=P)).then_inc(vectors_loaded, 16)
                r += k
            assert r == NCOLS - C_NMIX
            load_in(0, 0)
            for t in range(TH, NT):
                sp.dma_start(x_in[:, t, :], x_v[t]).then_inc(x_loaded[t], 16)
            load_in(1, 1)
            with sp.Fori(0, (KT - 2) // 2) as i:
                for j in range(2):
                    raw_free(i * 2 + (2 + j))
                    load_in(j, i * 2 + (2 + j))
            with sp.Fori(0, (KT - 2) // 2) as i:
                for j in range(2):
                    raw_free(i * 2 + (KT + j))
                    load_in(j, i * 2 + j)
            raw_free(2 * KT - 2)
            load_in(2 * KT - 2, KT - 2)
            raw_free(I_BOUT)
            for r in range(2):
                sp.dma_start(raw[r:r + 1, I_BOUT % 2, 0:D], b_out).then_inc(raw_loaded[I_BOUT % 2], 16)
            for i, n in enumerate(I_OUT[0]):
                raw_free(n)
                load_out(n, i)
                if i == 2:
                    sp.wait_ge(z_lo, KT)
                    sp.dma_start(x2[0], x_v[0:TH].rearrange("t p d -> p t d")).then_inc(x_again[0], 16)

            raw_free(I_IN_LAST)
            load_in(I_IN_LAST, KT - 1)

            def ffn_loads(h):
                F = I_FFN[h]
                for p in range(2):
                    raw_free(F + p)
                    load_pair(F + p, w_up_v, p * P, FF)
                if h == 1:
                    sp.wait_ge(added, NQ * TH)
                    for t in range(TH):
                        sp.dma_start(out_v[t], x2[0][:, t, :]).then_inc(stored, 16)
                with sp.Fori(0, (NQ - 1) // 2) as i:
                    for s in range(2):
                        n = F + 2 + 3 * s
                        for k in range(2):
                            raw_free(i * 6 + (n + k))
                            load_pair(n + k, w_up_v, i * (4 * P) + (2 * s + 2 + k) * P, FF)
                        raw_free(i * 6 + (n + 2))
                        load_down(n + 2, i * 4 + 2 * s)

            ffn_loads(0)
            for i in range(2):
                raw_free(I_OUT[1][i])
                load_out(I_OUT[1][i], i)
            raw_free(I_DOWN_LAST)
            load_down(I_DOWN_LAST, 2 * (NQ - 1))
            sp.wait_ge(z_lo, 2 * KT)
            sp.dma_start(x2[1], x_v[TH:NT].rearrange("t p d -> p t d")).then_inc(x_again[1], 16)
            for i in range(2, 4):
                raw_free(I_OUT[1][i])
                load_out(I_OUT[1][i], i)
            ffn_loads(1)
            raw_free(I_END)
            load_down(I_END, 2 * (NQ - 1))
            for t in range(TH):
                sp.wait_ge(added, (2 * NQ - 1) * TH + t + 1)
                sp.dma_start(out_v[TH + t], x2[1][:, t, :]).then_inc(stored, 16)
            sp.wait_ge(stored, 16 * NT)

        @block.gpsimd
        def _(pool):
            nc.gpsimd.memset(ident[:, :], 0.0).then_inc(ident_zero, 1)
            nc.gpsimd.memset(ones[:, :], 1.0 / D).then_inc(ones_ready, 1)
            nc.gpsimd.memset(one_rows[:, :].bitcast(F32), 1.0).then_inc(ones_ready, 1)
            nc.gpsimd.memset(eps, EPS).then_inc(ones_ready, 1)
            pool.wait_ge(ident_zero, 1)
            nc.gpsimd.affine_select(out=ident[:, :], in_=ident[:, :], compare_op=ALU.not_equal, fill=1.0,
                                    base=0, pattern=[[-1, P]], channel_multiplier=1).then_inc(ident_ready, 1)
            nc.gpsimd.memset(u[0][:, :, 0:PAD], 0.0).then_inc(pad_ready, 1)

            dwr = dw.rearrange("j (t c) -> (j t) c", c=P)
            ffr = ff_dw.rearrange("j (t c) -> (j t) c", c=P)
            ffb = ff_dw_b.rearrange("o (t c) -> (o t) c", c=P)
            R1, R2 = P, TAPS * KT - P
            for dst, src in ((rows[0:R1, 0, :], dwr[0:R1]), (rows[0:R2, 1, :], dwr[R1:R1 + R2]),
                             (rows[0:4 * NP, 2, :], ffr[0:4 * NP]), (rows[0:2 * NP, 3, :], ffr[4 * NP:6 * NP]),
                             (rows[2 * NP:4 * NP, 3, :], ffb)):
                pool.dma_start(dst, src).then_inc(taps_loaded, 16)

            def split_lo(n, lo, src, hi):
                pool.wait_ge(raw_hi, n + 1)
                nc.gpsimd.tensor_tensor(lo, src, hi.bitcast(F32), ALU.subtract).then_inc(raw_lo, 1)

            def split_slot(n, par, slot):
                split_lo(n, wsp[:, slot, LO, :], raw[:, par % 2, :], wsp[:, slot, HI, :])

            def split_down(n, par):
                split_lo(n, wd[:, LO, :], raw[:, par % 2, :], wd[:, HI, :])

            def tap(unit, j, turn=0):
                c, h = POOL_UNITS[unit]
                pool.wait_ge(prod_ready, turn * TAPS_A_TURN + (PROD0[unit] + j + 1))
                if unit or j > 1:
                    pool.wait_ge(pool_tap, turn * TAPS_A_TURN + (TAP0[unit] + j - 1))
                before = ring[:, 0, :] if j == 1 else acc_sum[:, :]
                dst = u[h][:, c, PAD:] if j == TAPS - 1 else acc_sum[:, :]
                nc.gpsimd.tensor_tensor(dst, before, ring[:, j % RING, :], ALU.add).then_inc(pool_tap, 1)

            def taps(first, last):
                for i in range(first, last):
                    unit = sum(i >= p for p in PROD0[1:])
                    if i > PROD0[unit]:
                        if i == PROD0[MIXED + 1] + 1:
                            pool.wait_ge(conv_joined, LOOP_JOINED)
                        tap(unit, i - PROD0[unit])

            def item_out(h, i):
                split_slot(I_OUT[h][i], I_OUT[h][i], out_slot(h, i))

            for n in range(2 * KT - 1):
                split_slot(n, n, n % 2)
                if n < 2 * KT - 2:
                    taps(tap_cut(n - 1), tap_cut(n))
            U2 = PROD0[MIXED + 1]
            taps(tap_cut(2 * KT - 3), U2)
            split_lo(I_BOUT, b_rows[:, :], raw[0:2, I_BOUT % 2, 0:D], b_hi[:, :])
            item_out(0, 0)
            taps(U2, U2 + 6)
            item_out(0, 1)
            taps(U2 + 6, U2 + 13)
            item_out(0, 2)
            taps(U2 + 13, U2 + 18)
            item_out(0, 3)
            taps(U2 + 18, U2 + 23)
            split_slot(I_IN_LAST, I_IN_LAST, 1)
            taps(U2 + 23, U2 + TAPS)
            split_slot(F0, F0, 0)

            def sum_tile(c, n, other=None):
                s, value = unit_at[(c, 1)]
                pool.wait_ge(s, value)
                if n > 1:
                    pool.wait_ge(summed, n - 1)
                before = tile_sum if other is None else u[1][:, other, PAD:]
                nc.gpsimd.tensor_tensor(tile_sum, before, u[1][:, c, PAD:], ALU.add).then_inc(summed, 1)

            def sum_squares(k0, k1):
                for k in range(k0, k1):
                    pool.wait_ge(sq_done, KT + k + 1)
                    if k > 1:
                        pool.wait_ge(sq_summed, k - 1)
                    before = squares[1][0] if k == 1 else acc_sum[:, :]
                    nc.gpsimd.tensor_tensor(acc_sum[:, :], before, squares[1][k], ALU.add).then_inc(sq_summed, 1)

            def split_group(n, i=0, last=False):
                split_down(i * 6 + (n + 2), n + 2)
                split_slot(i * 6 + (n + 3), n + 3, 0)
                if not last:
                    split_slot(i * 6 + (n + 4), n + 4, 1)

            split_slot(F0 + 1, F0 + 1, 1)
            taps(PROD0[3], PROD0[3] + TAPS_BEFORE // 2)
            split_slot(F0 + 2, F0 + 2, 0)
            taps(PROD0[3] + TAPS_BEFORE // 2, PROD0[3] + TAPS_BEFORE)
            split_slot(F0 + 3, F0 + 3, 1)
            sum_tile(1, 1, 0)
            sum_tile(2, 2)
            with pool.Fori(0, NI) as i:
                for s in range(2):
                    split_group(F0 + 2 + 3 * s, i)
                    for j in range(TAPS_A_TURN // 2):
                        tap(3, TAPS_BEFORE + s * (TAPS_A_TURN // 2) + j, i)
            for j in range(TAPS_BEFORE + NI * TAPS_A_TURN, TAPS):
                tap(3, j)
            sum_tile(3, 3 + NI)
            split_down(last0 - 4, last0 - 4)
            sum_squares(1, 4)
            split_slot(last0 - 3, last0 - 3, 0)
            sum_squares(4, KT)
            split_slot(last0 - 2, last0 - 2, 1)
            split_group(last0 - 3)
            split_down(I_DOWN_LAST, I_DOWN_LAST)
            item_out(1, 2)
            item_out(1, 3)
            for n in range(4):
                split_slot(F1 + n, F1 + n, n % 2)
            with pool.Fori(0, (NQ - 3) // 2) as i:
                for s in range(2):
                    split_group(F1 + 2 + 3 * s, i)
            split_group(I_END - 6)
            split_group(I_END - 3, last=True)

        @block.scalar
        def _(a):
            def split_hi(n, dst, src=None):
                item_ready(a, n)
                src = raw[:, n % 2, :] if src is None else src
                nc.scalar.activation(dst, src, ACT.Copy).then_inc(raw_hi, 1)

            def square(n_before, t, src, junk, waits):
                for w, value in waits:
                    a.wait_ge(w, value)
                if n_before:
                    a.wait_ge(squared, n_before)
                nc.scalar.activation(junk, src, ACT.Square, accum_out=ssq[:, t:t + 1]).then_inc(squared, 1)

            def root(h, n):
                a.wait_ge(squared, n)
                nc.scalar.activation(rms[:, h * TH:(h + 1) * TH], ssq[:, h * TH:(h + 1) * TH], ACT.Sqrt,
                                     bias=eps, scale=1.0 / D).then_inc(rms_ready, 1)

            def turned_hi(stage, slot, gain):
                for k in range(KT):
                    n = stage * KT + k
                    a.wait_ge(turned, n + 1)
                    nc.scalar.activation(hT[:, slot, HI, k, :], ps[:, B_T + n % 4, :], ACT.Copy,
                                         scale=col(gain + k)).then_inc(h_hi, 1)

            a.wait_ge(ones_ready, 3)
            a.wait_ge(pad_ready, 1)
            for t in range(TH):
                square(t, t, x_in[:, t, :], sig_flat, [(x_loaded[t], 16)])
            root(0, TH)
            split_hi(0, wsp[:, 0, HI, :])
            a.wait_ge(cols_ready, 1)
            turned_hi(0, 0, C_NMIX)
            for t in range(TH, NT):
                square(t, t, x_in[:, t, :], sig_flat, [(x_loaded[t], 16)])
            root(1, NT)
            split_hi(1, wsp[:, 1, HI, :])
            turned_hi(1, 1, C_NMIX)

            def sigmoid(n):
                a.wait_ge(g_done, n + 1)
                if n >= 2:
                    a.wait_ge(glu_done, n - 1)
                nc.scalar.activation(sig[:, n % 2, :], ps[:, B_G + n % 2, :], ACT.Sigmoid,
                                     bias=col(C_BIN + KT + n % KT)).then_inc(sig_done, 1)

            def product(unit, j, turn=0):
                c, h = POOL_UNITS[unit]
                if j == 0:
                    a.wait_ge(glu_done, h * KT + c + 1)
                if j >= RING:
                    a.wait_ge(pool_tap, turn * TAPS_A_TURN + (TAP0[unit] + max(j - RING, 1)))
                elif unit:
                    a.wait_ge(pool_tap, TAP0[unit])
                if j == 0:
                    ins = nc.scalar.activation(ring[:, 0, :], u[h][:, c, 0:HALF], ACT.Identity,
                                               scale=col(C_DW + c), bias=col(C_DWB + c))
                else:
                    src = u_all[:, bass.ds(turn * TAPS_A_TURN + ((h * KT + c) * W + j), HALF)]
                    w = cols[:, bass.ds(turn * (TAPS_A_TURN * KT) + (C_DW + j * KT + c), 1)]
                    ins = nc.scalar.activation(ring[:, j % RING, :], src, ACT.Copy, scale=w)
                ins.then_inc(prod_ready, 1)

            product_at = [0]

            def products(count):
                for i in range(product_at[0], product_at[0] + count):
                    unit = sum(i >= p for p in PROD0[1:])
                    product(unit, i - PROD0[unit])
                product_at[0] += count

            a.wait_ge(squared, NT)
            for n in range(2 * KT - 2):
                if n:
                    a.wait_ge(a_done, n)
                    split_hi(n + 1, wsp[:, (n + 1) % 2, HI, :])
                sigmoid(n)
                if n < 2 * KT - 3 and tap_cut(n + 1):
                    products(tap_cut(n + 1) + 1 - product_at[0])
            products(PROD0[2] - product_at[0])
            split_hi(I_BOUT, b_hi[:, :], raw[0:2, I_BOUT % 2, 0:D])
            a.wait_ge(a_done, 2 * KT - 2)
            split_hi(I_OUT[0][0], wsp[:, out_slot(0, 0), HI, :])
            a.wait_ge(raw_lo, I_BOUT + 1)
            nc.scalar.activation(b_rows[0:1, :], b_hi[0:1, :].bitcast(F32), ACT.Copy).then_inc(b_ready, 1)
            products(3)

            def square_tiles(h, k0, k1):
                for k in range(k0, k1):
                    n = h * KT + k
                    a.wait_ge(centred, n + 1)
                    if h and k >= 4:
                        a.wait_ge(sq_summed, max(k - 4, 1))
                    nc.scalar.activation(squares[h][k], u[h][:, conv_order[h][k], PAD:], ACT.Square).then_inc(sq_done, 1)

            def deviation(h):
                a.wait_ge(var_added, (KT, KT + 1)[h])
                nc.scalar.activation(norm[h][:, N_STD, :], ps[:, B_VAR[h], :], ACT.Sqrt, bias=eps).then_inc(std_done, 1)

            def silus(h, k0, k1):
                def silu(k, dst, signal):
                    nc.scalar.activation(dst, u[h][:, k, PAD:], ACT.Silu, scale=col(C_LNG + k),
                                         bias=col(C_LNB + k)).then_inc(signal, 1)

                for k in range(k0, k1 + 1):
                    if k < k1:
                        a.wait_ge(scaled, h * KT + k + 1)
                        silu(k, hT[:, 0, HI, k, :], z_hi)
                    if k > k0:
                        a.wait_ge(z_hi, h * KT + k)
                        silu(k - 1, u[h][:, k - 1, PAD:], z_full)

            square_tiles(0, 0, KT)
            deviation(0)
            products(2)
            sigmoid(2 * KT - 2)
            silus(0, 0, KT // 2)
            a.wait_ge(a_done, 2 * KT - 1)
            products(1)
            split_hi(I_OUT[0][1], wsp[:, out_slot(0, 1), HI, :])
            silus(0, KT // 2, KT)
            products(7)
            a.wait_ge(out_read, 1)
            split_hi(I_OUT[0][2], wsp[:, out_slot(0, 2), HI, :])
            products(5)
            a.wait_ge(out_done, TH)
            split_hi(I_OUT[0][3], wsp[:, out_slot(0, 3), HI, :])
            products(5)
            a.wait_ge(out_read, 2)
            split_hi(I_IN_LAST, wsp[:, 1, HI, :])

            def ffn_input(h):
                for t in range(TH):
                    square(NT + h * TH + t, h * TH + t, x2[h][:, t, :], junk[h], [(x2_done, (h * DH + 1) * TH + t + 1)])
                    if h == 0:
                        products(2)
                root(h, NT + (h + 1) * TH)
                if h == 0:
                    split_hi(F0, wsp[:, 0, HI, :])
                    sigmoid(2 * KT - 1)
                else:
                    split_hi(F1 + 1, wsp[:, 1, HI, :])
                turned_hi(2 + h, 1, C_NFFN)
                if h == 0:
                    a.wait_ge(a_done, 2 * KT)
                    split_hi(F0 + 1, wsp[:, 1, HI, :])

            def pair(h, p, par, slot, down_next=None, own_next=None, inside=lambda: None):
                n = p + h * NP
                for g, bank, done, dst, first, free in ((0, B_UPG, upg_done, y_g, g_first, prod_done),
                                                        (1, B_UPV, upv_done, y_v, v_first, act_lo)):
                    a.wait_ge(done, n + 1)
                    f = p + g * NP
                    if h == 0:
                        nc.scalar.activation(tails[:, bass.ds(f * 2, 2)], ps[:, bank, HALF - 2:], ACT.Copy)
                    if not (isinstance(n, int) and n == 0):
                        a.wait_ge(free, n)
                    nc.scalar.activation(dst[:, :], ps[:, bank, :], ACT.Identity,
                                         scale=cols[:, bass.ds(f + (C_FF + 2 * 2 * NP), 1)],
                                         bias=cols[:, bass.ds(f + (C_FF + 3 * 2 * NP), 1)]).then_inc(first, 1)
                    if g == 0:
                        split_item(down_next, wd[:, HI, :])
                        inside()
                a.wait_ge(g_taps, n + 1)
                nc.scalar.activation(y_g[:, :], y_g[:, :], ACT.Silu).then_inc(silu_done, 1)
                a.wait_ge(prod_done, n + 1)
                nc.scalar.activation(act[:, slot, par, HI, :], y_v[:, :], ACT.Copy).then_inc(act_hi, 1)
                split_item(own_next, wsp[:, par, HI, :])

            def split_item(what, dst):
                if what is not None:
                    count, n = what
                    a.wait_ge(raw_loaded[n % 2], count)
                    nc.scalar.activation(dst, raw[:, n % 2, :], ACT.Copy).then_inc(raw_hi, 1)

            def item(n, i=0):
                return i * 96 + (n // 2 + 1) * 32, n

            def group(h, q, s, i=0, inside=(lambda: None,) * 2, between=lambda: None, last=False):
                n = I_FFN[h] + 2 + 3 * s
                pair(h, q * 2, 0, (s + 1) % 2, down_next=item(n + 2, i), own_next=item(n + 3, i),
                     inside=inside[0])
                between()
                pair(h, q * 2 + 1, 1, (s + 1) % 2, own_next=None if last else item(n + 4, i), inside=inside[1])

            def first_pair(h, p, inside=lambda: None):
                pair(h, p, p, 0, own_next=item(I_FFN[h] + 2 + p), inside=inside)

            ffn_input(0)
            for p in range(2):
                first_pair(0, p, lambda: products(TAPS_BEFORE // 2))
            with a.Fori(0, NI) as i:
                for s in range(2):
                    group(0, i * 2 + (s + 1), s, i)
                    for j in range(TAPS_A_TURN // 2):
                        product(3, TAPS_BEFORE + s * (TAPS_A_TURN // 2) + j, i)
            for j in range(TAPS_BEFORE + NI * TAPS_A_TURN, TAPS):
                product(3, j)
            group(0, NQ - 2, 2 * NI, 0, (lambda: square_tiles(1, 0, 4), lambda: None),
                  lambda: square_tiles(1, 4, KT))
            deviation(1)
            group(0, NQ - 1, 2 * NI + 1, 0, (lambda: silus(1, 0, 2), lambda: silus(1, 3, 5)),
                  lambda: silus(1, 2, 3))
            silus(1, 5, KT)
            a.wait_ge(down_done, (NQ - 1) * TH)
            split_hi(I_DOWN_LAST, wd[:, HI, :])
            a.wait_ge(out_read, 3)
            split_hi(I_OUT[1][2], wsp[:, out_slot(1, 2), HI, :])
            a.wait_ge(out_done, 3 * TH)
            split_hi(I_OUT[1][3], wsp[:, out_slot(1, 3), HI, :])
            a.wait_ge(out_read, 4)
            split_hi(F1, wsp[:, 0, HI, :])
            ffn_input(1)
            for p in range(2):
                first_pair(1, p)
            with a.Fori(0, (NQ - 3) // 2) as i:
                for s in range(2):
                    group(1, i * 2 + (s + 1), s, i)
            group(1, NQ - 2, NQ - 3)
            group(1, NQ - 1, NQ - 2, last=True)

        @block.vector
        def _(dve):
            v = nc.vector

            def diagonals(stage, h, waits):
                dve.wait_ge(rms_ready, stage + 1)
                v.reciprocal(rrms[:, h * TH:(h + 1) * TH], rms[:, h * TH:(h + 1) * TH]).then_inc(rrms_ready, 1)
                for w, value in waits:
                    dve.wait_ge(w, value)
                dve.wait_ge(rrms_ready, stage + 1)
                for t in range(TH):
                    ins = v.tensor_scalar(diag[:, t * P:(t + 1) * P], ident[:, :],
                                          rrms[:, h * TH + t:h * TH + t + 1], None, ALU.mult)
                ins.then_inc(diag_ready, 1)

            def turned_lo(stage, slot, gain):
                for k in range(KT):
                    n = stage * KT + k
                    dve.wait_ge(h_hi, n + 1)
                    v.scalar_tensor_tensor(out=hT[:, slot, LO, k, :], in0=ps[:, B_T + n % 4, :], scalar=col(gain + k),
                                           in1=hT[:, slot, HI, k, :].bitcast(F32), op0=ALU.mult,
                                           op1=ALU.subtract).then_inc(h_lo, 1)

            def glu(n):
                h, c = divmod(n, KT)
                dve.wait_ge(sig_done, n + 1)
                dve.wait_ge(a_done, n + 1)
                spots = [(u[h][:, c, PAD:], 0)]
                if h == 0:
                    spots.insert(0, (u[1][:, c, 0:PAD], HALF - PAD))
                for dst, s in spots:
                    ins = v.scalar_tensor_tensor(out=dst, in0=ps[:, B_A + n % 2, s:], scalar=col(C_BIN + c),
                                                 in1=sig[:, n % 2, s:], op0=ALU.add, op1=ALU.mult)
                ins.then_inc(glu_done, 1)

            taps_done = [0, 0]
            joined = [0]

            def conv(n, hooks=None):
                units = CHAINS[n]
                if len(units) == 2:
                    chains = [(unit, range(TAPS)) for unit in units]
                else:
                    chains = [(units[0], range(0, TAPS, 2)), (units[0], range(1, TAPS, 2))]
                for step in range(len(chains[0][1])):
                    for i, ((c, h), taps) in enumerate(chains):
                        if step >= len(taps):
                            continue
                        j = taps[step]
                        if taps_done[i]:
                            dve.wait_ge(tap_done[i], taps_done[i])
                        if step == 0:
                            dve.wait_ge(glu_done, h * KT + c + 1)
                        if step == 0 and joined[0]:
                            dve.wait_ge(conv_joined, joined[0])
                        acc = ps[:, B_CONV + i, :]
                        src, w = u[h][:, c, j:j + HALF], col(C_DW + j * KT + c)
                        if j == 0:
                            ins = v.tensor_scalar(acc, src, w, col(C_DWB + c), ALU.mult, ALU.add)
                        elif step == 0:
                            ins = v.tensor_scalar(acc, src, w, None, ALU.mult)
                        else:
                            dst = src if j == TAPS - 1 else acc
                            if j == TAPS - 1 and len(units) == 1:
                                dve.wait_ge(tap_done[1], taps_done[1])
                            ins = v.scalar_tensor_tensor(out=dst, in0=src, scalar=w, in1=acc,
                                                         op0=ALU.mult, op1=ALU.add)
                        ins.then_inc(tap_done[i], 1)
                        taps_done[i] += 1
                    for work in (hooks or {}).get(step, ()):
                        work()
                if len(units) == 1:
                    c, h = units[0]
                    dve.wait_ge(tap_done[0], taps_done[0])
                    v.tensor_tensor(u[h][:, c, PAD:], u[h][:, c, PAD:], ps[:, B_CONV + 1, :],
                                    ALU.add).then_inc(conv_joined, 1)
                    joined[0] += 1

            def centre(h):
                dve.wait_ge(mean_done, h + 1)
                for c in conv_order[h]:
                    v.tensor_tensor(u[h][:, c, PAD:], u[h][:, c, PAD:], ps[:, B_MEAN[h], :],
                                    ALU.subtract).then_inc(centred, 1)

            def invert(h):
                dve.wait_ge(std_done, h + 1)
                v.reciprocal(norm[h][:, N_RSTD, :], norm[h][:, N_STD, :]).then_inc(rstd_done, 1)

            def scale(h):
                dve.wait_ge(rstd_done, h + 1)
                for k in range(KT):
                    v.tensor_tensor(u[h][:, k, PAD:], u[h][:, k, PAD:], norm[h][:, N_RSTD, :], ALU.mult).then_inc(scaled, 1)

            def z_low(h, k0, k1):
                for k in range(k0, k1):
                    dve.wait_ge(z_full, h * KT + k + 1)
                    v.tensor_tensor(hT[:, 0, LO, k, :], u[h][:, k, PAD:], hT[:, 0, HI, k, :].bitcast(F32),
                                    ALU.subtract).then_inc(z_lo, 1)

            def add_out(h, i):
                d, t = divmod(i, TH)
                dve.wait_ge(out_done, h * DH * TH + i + 1)
                dve.wait_ge(x_again[h], 16)
                x2_t = x2[h][:, t, d * 512:(d + 1) * 512]
                v.tensor_tensor(x2_t, x2_t, ps[:, t, :], ALU.add).then_inc(x2_done, 1)

            def copy_cols(n, c0, c1):
                dve.wait_ge(cols_turned, n + 1)
                v.tensor_copy(cols[:, c0:c1], ps[:, B_COLS[n], c0:c1]).then_inc(cols_ready, 1)

            copy_cols(0, C_NMIX, NCOLS)
            dve.wait_ge(ident_ready, 1)
            diagonals(0, 0, [(cols_ready, 1)])
            turned_lo(0, 0, C_NMIX)
            copy_cols(1, 0, C_NMIX)
            diagonals(1, 1, [(turned, KT)])
            turned_lo(1, 1, C_NMIX)
            glu(0)
            dve.wait_ge(pad_ready, 1)

            def at(first, every, works):
                return {first + every * i: [w] for i, w in enumerate(works)}

            def glus(a, b):
                return [lambda n=n: glu(n) for n in range(a, b)]

            def mixed(n):
                c, h = POOL_UNITS[MIXED]
                j = MIXED_FROM + n
                acc, src, w = ps[:, B_MIXED, :], u[h][:, c, j:j + HALF], col(C_DW + j * KT + c)
                if n == 0:
                    ins = v.tensor_scalar(acc, src, w, None, ALU.mult)
                else:
                    dve.wait_ge(mixed_tap, n)
                    ins = v.scalar_tensor_tensor(out=acc, in0=src, scalar=w, in1=acc, op0=ALU.mult, op1=ALU.add)
                ins.then_inc(mixed_tap, 1)

            def join_mixed():
                c, h = POOL_UNITS[MIXED]
                dve.wait_ge(mixed_tap, TAPS - MIXED_FROM)
                dve.wait_ge(pool_tap, TAP0[MIXED + 1])
                v.tensor_tensor(u[h][:, c, PAD:], ps[:, B_MIXED, :], acc_sum[:, :], ALU.add).then_inc(conv_joined, 1)
                joined[0] += 1

            conv(0, at(4, 8, glus(1, 3)))
            conv(1, at(4, 8, glus(3, 5)))
            conv(2, at(5, 8, glus(5, 9)))
            hooks = at(4, 7, glus(9, 13))
            for n in range(TAPS - MIXED_FROM):
                hooks.setdefault(1 + 4 * n, []).append(lambda n=n: mixed(n))
            conv(3, hooks)
            glu(2 * KT - 3)
            join_mixed()
            centre(0)
            invert(0)
            scale(0)
            z_low(0, 0, KT // 2)
            glu(2 * KT - 2)
            z_low(0, KT // 2, KT)
            adds = [lambda n=n: add_out(0, n) for n in range(DH * TH)]
            conv(4, {**at(7, 2, adds[:TH]), **at(20, 2, adds[TH:])})

            def ffn_input(h, adds):
                for work in adds[:1]:
                    work()
                diagonals(2 + h, h, [(turned, (2 + h) * KT)])
                for work in adds[1:]:
                    work()
                turned_lo(2 + h, 1, C_NFFN)

            def later_taps(h, p, g, bank, y, first, second, done):
                n = p + h * NP
                f = p + g * NP
                w1 = cols[:, bass.ds(f + (C_FF + 2 * NP), 1)]
                w0 = cols[:, bass.ds(f + C_FF, 1)]
                dve.wait_ge(first, n + 1)

                def tap(dst, src, w):
                    return v.scalar_tensor_tensor(out=dst, in0=src, scalar=w, in1=dst, op0=ALU.mult, op1=ALU.add)

                if h:
                    tap(y[:, 0:1], tails[:, bass.ds(f * 2 + 1, 1)], w1)
                tap(y[:, 1:], ps[:, bank, 0:HALF - 1], w1).then_inc(second, 1)
                dve.wait_ge(second, n + 1)
                if h:
                    tap(y[:, 0:2], tails[:, bass.ds(f * 2, 2)], w0)
                tap(y[:, 2:], ps[:, bank, 0:HALF - 2], w0).then_inc(done, 1)

            def add_down(h, n, t):
                dve.wait_ge(down_done, n + 1)
                v.tensor_tensor(x2[h][:, t, :], x2[h][:, t, :], banks(B_DOWN + 2 * (t % 2)), ALU.add).then_inc(added, 1)

            def pair(h, p, par, slot, down_of=None, conv_taps=lambda n: None, inside=lambda: None):
                n = p + h * NP
                adds = [] if down_of is None else list(range(TH))

                def add():
                    if adds:
                        t = adds.pop(0)
                        add_down(h, down_of * TH + t, t)

                later_taps(h, p, 0, B_UPG, y_g, g_first, g_second, g_taps)
                conv_taps(4)
                inside()
                later_taps(h, p, 1, B_UPV, y_v, v_first, v_second, v_taps)
                dve.wait_ge(silu_done, n + 1)
                dve.wait_ge(v_taps, n + 1)
                v.tensor_tensor(y_v[:, :], y_g[:, :], y_v[:, :], ALU.mult).then_inc(prod_done, 1)
                add()
                dve.wait_ge(act_hi, n + 1)
                v.tensor_tensor(act[:, slot, par, LO, :], y_v[:, :], act[:, slot, par, HI, :].bitcast(F32),
                                ALU.subtract).then_inc(act_lo, 1)
                while adds:
                    add()
                conv_taps(4)

            def group(h, q, s, conv_taps=lambda n: None, inside=(lambda: None,) * 2, between=lambda: None):
                pair(h, q * 2, 0, (s + 1) % 2, conv_taps=conv_taps, inside=inside[0])
                between()
                pair(h, q * 2 + 1, 1, (s + 1) % 2, down_of=q + (h * NQ - 1), conv_taps=conv_taps, inside=inside[1])

            ffn_input(0, [lambda: None, lambda: glu(2 * KT - 1)])
            pair(0, 0, 0, 0)
            pair(0, 1, 1, 0)
            with dve.Fori(0, NI) as i:
                next_tap = [0]

                def conv_taps(count):
                    for j in range(next_tap[0], min(next_tap[0] + count, TAPS)):
                        e = j % 2
                        per_turn = (TAPS + 1 - e) // 2
                        dve.wait_ge(tap_done[e], i * per_turn + (LOOP_TAPS[e] + j // 2))
                        if j < 2:
                            dve.wait_ge(conv_joined, i + LOOP_JOINED)
                        acc = ps[:, B_LOOP + e, :]
                        src = u_all[:, bass.ds(i * W + ((KT + LOOP_FIRST) * W + j), HALF)]
                        w = cols[:, bass.ds(i + (C_DW + j * KT + LOOP_FIRST), 1)]
                        if j == 0:
                            ins = v.tensor_scalar(acc, src, w, cols[:, bass.ds(i + (C_DWB + LOOP_FIRST), 1)],
                                                  ALU.mult, ALU.add)
                        elif j == 1:
                            ins = v.tensor_scalar(acc, src, w, None, ALU.mult)
                        else:
                            if j == TAPS - 1:
                                dve.wait_ge(tap_done[1], i * (TAPS // 2) + (LOOP_TAPS[1] + TAPS // 2))
                            ins = v.scalar_tensor_tensor(out=src if j == TAPS - 1 else acc, in0=src, scalar=w,
                                                         in1=acc, op0=ALU.mult, op1=ALU.add)
                        ins.then_inc(tap_done[e], 1)
                        if j == TAPS - 1:
                            dve.wait_ge(tap_done[0], i * per_turn + (LOOP_TAPS[0] + per_turn))
                            v.tensor_tensor(src, src, ps[:, B_LOOP + 1, :], ALU.add).then_inc(conv_joined, 1)
                            dve.wait_ge(conv_joined, i + (LOOP_JOINED + 1))
                            dve.wait_ge(summed, i + 2)
                            v.tensor_tensor(tile_sum, tile_sum, src, ALU.add).then_inc(summed, 1)
                    next_tap[0] += count

                for s in range(2):
                    group(0, i * 2 + (s + 1), s, conv_taps)
            group(0, NQ - 2, 2 * NI, inside=(lambda: centre(1), lambda: None))
            invert(1)
            group(0, NQ - 1, 2 * NI + 1, inside=(lambda: scale(1), lambda: z_low(1, 2, 4)),
                  between=lambda: z_low(1, 0, 2))
            z_low(1, 4, KT)
            for n in range(DH * TH):
                add_out(1, n)
            ffn_input(1, [lambda t=t: add_down(0, (NQ - 1) * TH + t, t) for t in range(TH)])
            pair(1, 0, 0, 0)
            pair(1, 1, 1, 0)
            with dve.Fori(0, (NQ - 1) // 2) as i:
                for s in range(2):
                    group(1, i * 2 + (s + 1), s)
            for t in range(TH):
                add_down(1, (2 * NQ - 1) * TH + t, t)

        @block.tensor
        def _(pe):
            mm = nc.tensor.matmul
            PASSES = ((HI, HI), (HI, LO), (LO, HI))

            def turn(stage, src):
                pe.wait_ge(diag_ready, stage + 1)
                for k in range(KT):
                    n = stage * KT + k
                    if n >= 4:
                        pe.wait_ge(h_lo, n - 3)
                    if stage == 3 and k == 2:
                        pe.wait_ge(added, NQ * TH)
                    for t in range(TH):
                        ins = mm(ps[:, B_T + n % 4, t * P:(t + 1) * P], src[:, t, k * P:(k + 1) * P],
                                 diag[:, t * P:(t + 1) * P], start=True, stop=True)
                    ins.then_inc(turned, 1)

            def project(bank, slot, g, x_slot, signal, each=None):
                for k in range(KT):
                    if each is not None:
                        pe.wait_ge(h_lo, each + k + 1)
                    for n, (pw, px) in enumerate(PASSES):
                        ins = mm(ps[:, bank, :], wtile(slot, pw, k, g), hT[:, x_slot, px, k, :],
                                 start=(k == 0 and n == 0), stop=(k == KT - 1 and n == 2))
                ins.then_inc(signal, 1)

            def in_pair(n, par, h, item_=None, after=None):
                pe.wait_ge(raw_lo, (n if item_ is None else item_) + 1)
                for i, (bank, g, free, signal) in enumerate(((B_G, 0, sig_done, g_done), (B_A, 1, glu_done, a_done))):
                    if after is None:
                        pe.wait_ge(free, n - 1)
                    else:
                        pe.wait_ge(*after[i])
                    project(bank + par, par, g, h, signal)

            def turn_rows(sets, bank, at):
                for r, k in sets:
                    ins = nc.tensor.transpose(ps[:, bank, at:at + k], rows[0:k, r, :], ident[0:k, 0:k])
                    at += k
                ins.then_inc(cols_turned, 1)

            pe.wait_ge(ident_ready, 1)
            pe.wait_ge(vectors_loaded, 6 * 16)
            turn_rows(((4, NCOLS - C_NMIX), ), B_COLS[0], C_NMIX)

            pe.wait_ge(ones_ready, 3)
            for n in range(2):
                turn(n, x_in[:, n * TH:(n + 1) * TH, :])
                if n == 0:
                    pe.wait_ge(taps_loaded, 5 * 16)
                    turn_rows(((0, P), (1, TAPS * KT - P), (2, 4 * NP), (3, 4 * NP)), B_COLS[1], 0)
                pe.wait_ge(cols_ready, n + 1)
                pe.wait_ge(raw_lo, n + 1)
                project(B_G + n, n, 0, 0, g_done, each=n * KT)
                project(B_A + n, n, 1, 0, a_done)
            with pe.Fori(2, KT, 2) as n:
                in_pair(n, 0, 0)
                in_pair(n + 1, 1, 0)
            with pe.Fori(KT, 2 * KT - 2, 2) as n:
                in_pair(n, 0, 1)
                in_pair(n + 1, 1, 1)

            def statistics():
                for n, c in enumerate(conv_order[0]):
                    s, value = unit_at[(c, 0)]
                    pe.wait_ge(s, value)
                    ins = mm(ps[:, B_MEAN[0], :], ones[:, :], u[0][:, c, PAD:], start=(n == 0), stop=(n == KT - 1))
                ins.then_inc(mean_done, 1)
                for k in range(KT):
                    pe.wait_ge(sq_done, k + 1)
                    mm(ps[:, B_VAR[0], :], ones[:, :], squares[0][k], start=(k == 0),
                       stop=(k == KT - 1)).then_inc(var_added, 1)

            def mean_of_sum():
                pe.wait_ge(summed, 3 + NI)
                mm(ps[:, B_MEAN[1], :], ones[:, :], tile_sum, start=True, stop=True).then_inc(mean_done, 1)

            def variance_of_sum():
                pe.wait_ge(sq_summed, KT - 1)
                mm(ps[:, B_VAR[1], :], ones[:, :], acc_sum[:, :], start=True, stop=True).then_inc(var_added, 1)

            def project_out(h):
                for i, n in enumerate(I_OUT[h]):
                    d, kh = divmod(i, 2)
                    pe.wait_ge(raw_lo, n + 1)
                    for t in range(TH):
                        if d and not kh:
                            pe.wait_ge(x2_done, h * DH * TH + t + 1)
                        elif h == 0 and not kh:
                            pe.wait_ge((sig_done, glu_done)[t // 2], 2 * KT - 1 - t % 2)
                        if t == 0 and d == 0:
                            pe.wait_ge(z_lo, h * KT + (kh + 1) * KT // 2)
                        for k in range(KT // 2):
                            for m, (pz, pw) in enumerate(PASSES):
                                ins = mm(ps[:, t, :], hT[:, 0, pz, kh * KT // 2 + k, t * P:(t + 1) * P],
                                         wsp[:, out_slot(h, i), pw, k * 512:(k + 1) * 512],
                                         start=(not kh and k == 0 and m == 0), stop=False)
                        if t == TH - 1 and not kh:
                            ins.then_inc(out_read, 1)
                        if kh:
                            pe.wait_ge(b_ready, 1)
                            mm(ps[:, t, :], one_rows[:, :], b_rows[:, d * 512:(d + 1) * 512],
                               start=False, stop=True).then_inc(out_done, 1)

            statistics()
            in_pair(2 * KT - 2, 0, 1)
            project_out(0)
            in_pair(2 * KT - 1, 1, 1, I_IN_LAST, ((x2_done, DH * TH - 2), (x2_done, DH * TH)))

            def down(n, slot, weights, t_free=2):
                pe.wait_ge(act_lo, n * 2 + 2)
                for t in range(TH):
                    if t >= t_free:
                        pe.wait_ge(added, n * TH + (t - 1))
                    for b in range(DH):
                        for k in range(2):
                            for m, (pa, pw) in enumerate(PASSES):
                                o = k * D + b * 512
                                ins = mm(ps[:, B_DOWN + 2 * (t % 2) + b, :], act[:, slot, k, pa, t * P:(t + 1) * P],
                                         weights(pw, o), start=(k == 0 and m == 0), stop=(k == 1 and m == 2))
                    ins.then_inc(down_done, 1)

            def in_wd(part, o):
                return wd[:, part, o:o + 512]

            def up_pair(n, item_, slot, between=lambda: None):
                pe.wait_ge(raw_lo, item_ + 1)
                for bank, g, free, signal in ((B_UPG, 0, g_taps, upg_done), (B_UPV, 1, v_taps, upv_done)):
                    pe.wait_ge(free, n)
                    project(bank, slot, g, 1, signal)
                    if g == 0:
                        between()

            def group(h, q, item_, s, between=lambda: None):
                up_pair(q * 2 + h * NP, item_, 0, between)
                up_pair(q * 2 + (h * NP + 1), item_ + 1, 1)
                pe.wait_ge(raw_lo, item_ + 3)
                down(q + (h * NQ - 1), s % 2, in_wd)

            def first_pairs(h):
                turn(2 + h, x2[h])
                pe.wait_ge(x2_done, (h + 1) * DH * TH)
                pe.wait_ge(raw_lo, I_FFN[h] + 1)
                project(B_UPG, 0, 0, 1, upg_done, each=(2 + h) * KT)
                project(B_UPV, 0, 1, 1, upv_done)
                up_pair(h * NP + 1, I_FFN[h] + 1, 1)

            first_pairs(0)
            with pe.Fori(0, NI) as i:
                for s in range(2):
                    group(0, i * 2 + (s + 1), i * 6 + (F0 + 2 + 3 * s), s)
            for q, between in ((NQ - 2, mean_of_sum), (NQ - 1, lambda: None)):
                group(0, q, F0 + 2 + 3 * (q - 1), q - 1, between)
                if q == NQ - 2:
                    variance_of_sum()
            project_out(1)
            pe.wait_ge(raw_lo, I_DOWN_LAST + 1)
            pe.wait_ge(added, (NQ - 1) * TH)
            down(NQ - 1, 0, in_wd)
            pe.wait_ge(added, NQ * TH - 1)
            first_pairs(1)
            with pe.Fori(0, (NQ - 1) // 2) as i:
                for s in range(2):
                    group(1, i * 2 + (s + 1), i * 6 + (F1 + 2 + 3 * s), s)
            pe.wait_ge(raw_lo, I_END + 1)
            down(2 * NQ - 1, 0, lambda part, o: wsp[:, 0, part, o:o + 512], t_free=0)


_INS = ["x", "norm_mix", "norm_ffn", "cm_w_in", "cm_b_in", "cm_dw", "cm_dw_b", "cm_ln_g", "cm_ln_b",
        "cm_w_out", "cm_b_out", "ff_w_up", "ff_dw", "ff_dw_b", "ff_w_down"]


def kernel(**inputs):
    import numpy as np
    import concourse.bacc as bacc
    from concourse.bass_utils import run_bass_kernel_spmd

    nc = bacc.Bacc("TRN2", target_bir_lowering=False, num_devices=1)
    arrays, args = {}, []
    for name in _INS:
        a = np.ascontiguousarray(inputs[name])
        arrays[f"in_{name}"] = a
        ap = nc.dram_tensor(f"in_{name}", a.shape, mybir.dt.from_np(a.dtype), kind="ExternalInput").ap()
        args.append(ap if len(a.shape) == 2 else ap.rearrange("o a b -> (o a) b"))
    shape = inputs["x"].shape
    out = nc.dram_tensor("out", shape, F32, kind="ExternalOutput").ap()
    conformer_ffn(nc, *args, out.rearrange("o a b -> (o a) b"))
    r = run_bass_kernel_spmd(nc, [arrays], core_ids=[0])
    return r.results[0]["out"]
```
